# Optimizing a Trainium2 kernel written in Bass

```python
import math
import jax, jax.numpy as jnp
from jax import lax
import numpy as np

D_MODEL = 1024
BATCH = 1
SEQ = 256
DEPTH = 2

N_MIXERS = 2
N_MAMBA = (DEPTH + 1) // 2
N_MOBA = DEPTH // 2

SSM_EXPAND = 2
SSM_D_INNER = SSM_EXPAND * D_MODEL
SSM_HEAD_DIM = 64
SSM_HEADS = SSM_D_INNER // SSM_HEAD_DIM
SSM_GROUPS = 8
SSM_HEADS_PER_GROUP = SSM_HEADS // SSM_GROUPS
SSM_STATE = 128
SSM_CONV = 4
SSM_CHUNK = 256
SSM_CONV_DIM = SSM_D_INNER + 2 * SSM_GROUPS * SSM_STATE
SSM_IN_DIM = SSM_D_INNER + SSM_CONV_DIM + SSM_HEADS

ATTN_HEAD_DIM = 64
ATTN_HEADS = D_MODEL // ATTN_HEAD_DIM
MOBA_BLOCK = 256
MOBA_TOPK = 3
MOBA_Q_CHUNK = 16
ALIBI_MAX_BIAS = 8.0

D_FF = 2816
RMS_EPS = 1e-6


def rmsnorm(x, g):
    xf = x.astype(jnp.float32)
    y = xf * lax.rsqrt(jnp.mean(xf * xf, axis=-1, keepdims=True) + RMS_EPS)
    return (y * g.astype(jnp.float32)).astype(x.dtype)

def modulate(x, g, c_act, w, b):
    m = c_act @ w + b
    shift, scale, gate = jnp.split(m, 3, axis=-1)
    h = rmsnorm(x, g) * (1.0 + scale[:, None, :]) + shift[:, None, :]
    return h, gate[:, None, :]

def swiglu(h, w_gate, w_up, w_down):
    return (jax.nn.silu(h @ w_gate) * (h @ w_up)) @ w_down

def ssd_chunked_scan(x, dt, a, bm, cm):
    bsz, L = x.shape[0], x.shape[1]
    n_chunks = -(-L // SSM_CHUNK)
    pad = n_chunks * SSM_CHUNK - L

    def to_chunks(t):
        t = jnp.pad(t.astype(jnp.float32), [(0, 0), (0, pad)] + [(0, 0)] * (t.ndim - 2))
        t = t.reshape((bsz, n_chunks, SSM_CHUNK) + t.shape[2:])
        return jnp.moveaxis(t, 1, 0)

    xc, dtc, bc, cc = to_chunks(x), to_chunks(dt), to_chunks(bm), to_chunks(cm)
    causal = jnp.tril(jnp.ones((SSM_CHUNK, SSM_CHUNK), dtype=bool))[None, :, :, None, None]

    def step(state, inp):
        x_k, dt_k, b_k, c_k = inp
        acum = jnp.cumsum(dt_k * a, axis=1)
        seg = acum[:, :, None] - acum[:, None, :]
        decay = jnp.exp(jnp.where(causal, seg, -jnp.inf))
        cb = jnp.einsum('btgn,bsgn->btsg', c_k, b_k)
        w = cb[..., None] * decay * dt_k[:, None]
        y_intra = jnp.einsum('btsgr,bsgrp->btgrp', w, x_k)
        y_inter = jnp.einsum('btgn,bgrpn->btgrp', c_k, state) * jnp.exp(acum)[..., None]
        to_end = jnp.exp(acum[:, -1:] - acum) * dt_k
        new_state = (state * jnp.exp(acum[:, -1])[..., None, None]
                     + jnp.einsum('bsgn,bsgr,bsgrp->bgrpn', b_k, to_end, x_k))
        return new_state, y_intra + y_inter

    state0 = jnp.zeros((bsz, SSM_GROUPS, SSM_HEADS_PER_GROUP, SSM_HEAD_DIM, SSM_STATE), jnp.float32)
    _, y = lax.scan(step, state0, (xc, dtc, bc, cc))
    y = jnp.moveaxis(y, 0, 1).reshape((bsz, n_chunks * SSM_CHUNK) + y.shape[3:])[:, :L]
    return y.astype(x.dtype)

def mamba2_mixer(h, w_in, conv_w, conv_b, dt_bias, a_log, d_skip, norm_w, w_out):
    bsz, L, _ = h.shape
    G, R, P, N = SSM_GROUPS, SSM_HEADS_PER_GROUP, SSM_HEAD_DIM, SSM_STATE
    proj = h @ w_in
    z, xbc, dt = jnp.split(proj, [SSM_D_INNER, SSM_D_INNER + SSM_CONV_DIM], axis=-1)
    xbc = lax.conv_general_dilated(
        xbc, conv_w, window_strides=(1,), padding=[(SSM_CONV - 1, 0)],
        dimension_numbers=('NWC', 'WIO', 'NWC'), feature_group_count=SSM_CONV_DIM) + conv_b
    xbc = jax.nn.silu(xbc)
    xs, bm, cm = jnp.split(xbc, [SSM_D_INNER, SSM_D_INNER + G * N], axis=-1)
    dt = jax.nn.softplus(dt.astype(jnp.float32) + dt_bias.astype(jnp.float32))
    a = -jnp.exp(a_log.astype(jnp.float32))
    xs = xs.reshape(bsz, L, G, R, P)
    y = ssd_chunked_scan(xs, dt.reshape(bsz, L, G, R), a.reshape(G, R),
                         bm.reshape(bsz, L, G, N), cm.reshape(bsz, L, G, N))
    y = y + d_skip.reshape(G, R)[..., None] * xs
    y = y.reshape(bsz, L, SSM_D_INNER)
    y = rmsnorm(y * jax.nn.silu(z), norm_w)
    return y @ w_out

def moba_mixer(h, w_qkv, w_out):
    bsz, L, _ = h.shape
    H, dh, BLK, QC = ATTN_HEADS, ATTN_HEAD_DIM, MOBA_BLOCK, MOBA_Q_CHUNK
    qkv = (h @ w_qkv).reshape(bsz, L, 3, H, dh)
    q = jnp.transpose(qkv[:, :, 0], (0, 2, 1, 3))
    k = jnp.transpose(qkv[:, :, 1], (0, 2, 1, 3))
    v = jnp.transpose(qkv[:, :, 2], (0, 2, 1, 3))
    n_blocks = -(-L // BLK)
    K = max(1, min(MOBA_TOPK, n_blocks))
    pad = n_blocks * BLK - L
    k = jnp.pad(k, [(0, 0), (0, 0), (0, pad), (0, 0)])
    v = jnp.pad(v, [(0, 0), (0, 0), (0, pad), (0, 0)])
    kb = k.reshape(bsz, H, n_blocks, BLK, dh)
    vb = v.reshape(bsz, H, n_blocks, BLK, dh)
    kmean = jnp.mean(kb.astype(jnp.float32), axis=3)
    scale = dh ** -0.5
    slopes = jnp.exp2(-ALIBI_MAX_BIAS * (jnp.arange(H, dtype=jnp.float32) + 1.0) / H)
    bi = jnp.arange(bsz)[:, None, None, None]
    hi = jnp.arange(H)[None, :, None, None]
    blk_ids = jnp.arange(n_blocks)
    in_blk = jnp.arange(BLK)

    def chunk(ci):
        q0 = ci * QC
        own = q0 // BLK
        qc = lax.dynamic_slice_in_dim(q, q0, QC, axis=2)
        qpos = q0 + jnp.arange(QC)
        gate = jnp.einsum('bhqd,bhnd->bhqn', qc.astype(jnp.float32), kmean)
        gate = jnp.where((blk_ids < own)[None, None, None, :], gate, -jnp.inf)
        _, sel = lax.top_k(gate, K)
        sel_valid = jnp.arange(K) < own
        k_sel = kb[bi, hi, sel]
        v_sel = vb[bi, hi, sel]
        kpos_sel = sel[..., None] * BLK + in_blk
        dist_sel = (qpos[:, None, None] - kpos_sel).astype(jnp.float32)
        s_sel = (jnp.einsum('bhqd,bhqkjd->bhqkj', qc, k_sel).astype(jnp.float32) * scale
                 - slopes[:, None, None, None] * dist_sel)
        s_sel = jnp.where(sel_valid[:, None], s_sel, -jnp.inf)
        k_own = lax.dynamic_slice_in_dim(k, own * BLK, BLK, axis=2)
        v_own = lax.dynamic_slice_in_dim(v, own * BLK, BLK, axis=2)
        kpos_own = own * BLK + in_blk
        dist_own = (qpos[:, None] - kpos_own[None, :]).astype(jnp.float32)
        s_own = (jnp.einsum('bhqd,bhjd->bhqj', qc, k_own).astype(jnp.float32) * scale
                 - slopes[:, None, None] * dist_own)
        s_own = jnp.where(dist_own >= 0.0, s_own, -jnp.inf)
        s = jnp.concatenate([s_own, s_sel.reshape(bsz, H, QC, K * BLK)], axis=-1)
        p = jax.nn.softmax(s, axis=-1).astype(v.dtype)
        p_own = p[..., :BLK]
        p_sel = p[..., BLK:].reshape(bsz, H, QC, K, BLK)
        return (jnp.einsum('bhqj,bhjd->bhqd', p_own, v_own)
                + jnp.einsum('bhqkj,bhqkjd->bhqd', p_sel, v_sel))

    out = lax.map(chunk, jnp.arange(L // QC))
    out = jnp.transpose(out, (1, 0, 3, 2, 4)).reshape(bsz, L, H * dh)
    return out @ w_out

def first_inputs(seed: int = 0) -> dict:
    key = jax.random.key(seed)
    ks = jax.random.split(key, 24)
    f32 = jnp.float32

    def nrm(k, shape, s):
        return jax.random.normal(k, shape, f32) * s

    x = nrm(ks[0], (BATCH, SEQ, D_MODEL), 1.0)
    c = nrm(ks[1], (BATCH, D_MODEL), 1.0)
    norm_g = 1.0 + nrm(ks[2], (DEPTH, 3, D_MODEL), 0.05)
    mod_w = nrm(ks[3], (DEPTH, 3, D_MODEL, 3 * D_MODEL), 0.5 * D_MODEL ** -0.5)
    mod_b = nrm(ks[4], (DEPTH, 3, 3 * D_MODEL), 0.02)
    ffn_w_gate = nrm(ks[5], (DEPTH, 2, D_MODEL, D_FF), D_MODEL ** -0.5)
    ffn_w_up = nrm(ks[6], (DEPTH, 2, D_MODEL, D_FF), D_MODEL ** -0.5)
    ffn_w_down = nrm(ks[7], (DEPTH, 2, D_FF, D_MODEL), D_FF ** -0.5)
    ssm_w_in = nrm(ks[8], (N_MAMBA, D_MODEL, SSM_IN_DIM), D_MODEL ** -0.5)
    ssm_conv_w = nrm(ks[9], (N_MAMBA, SSM_CONV, 1, SSM_CONV_DIM), SSM_CONV ** -0.5)
    ssm_conv_b = nrm(ks[10], (N_MAMBA, SSM_CONV_DIM), 0.02)
    dt0 = jnp.exp(jax.random.uniform(ks[11], (N_MAMBA, SSM_HEADS), f32,
                                     math.log(1e-3), math.log(1e-1)))
    ssm_dt_bias = dt0 + jnp.log(-jnp.expm1(-dt0))
    ssm_a_log = jnp.log(jax.random.uniform(ks[12], (N_MAMBA, SSM_HEADS), f32, 1.0, 16.0))
    ssm_d = 1.0 + nrm(ks[13], (N_MAMBA, SSM_HEADS), 0.05)
    ssm_norm_w = 1.0 + nrm(ks[14], (N_MAMBA, SSM_D_INNER), 0.05)
    ssm_w_out = nrm(ks[15], (N_MAMBA, SSM_D_INNER, D_MODEL), SSM_D_INNER ** -0.5)
    attn_w_qkv = nrm(ks[16], (N_MOBA, D_MODEL, 3 * D_MODEL), D_MODEL ** -0.5)
    attn_w_out = nrm(ks[17], (N_MOBA, D_MODEL, D_MODEL), D_MODEL ** -0.5)
    final_norm_g = 1.0 + nrm(ks[18], (D_MODEL,), 0.05)
    return {"x": x, "c": c, "norm_g": norm_g, "mod_w": mod_w, "mod_b": mod_b,
            "ffn_w_gate": ffn_w_gate, "ffn_w_up": ffn_w_up, "ffn_w_down": ffn_w_down,
            "ssm_w_in": ssm_w_in, "ssm_conv_w": ssm_conv_w, "ssm_conv_b": ssm_conv_b,
            "ssm_dt_bias": ssm_dt_bias, "ssm_a_log": ssm_a_log, "ssm_d": ssm_d,
            "ssm_norm_w": ssm_norm_w, "ssm_w_out": ssm_w_out,
            "attn_w_qkv": attn_w_qkv, "attn_w_out": attn_w_out,
            "final_norm_g": final_norm_g}

def first_block(x, c, norm_g, mod_w, mod_b, ffn_w_gate, ffn_w_up, ffn_w_down,
              ssm_w_in, ssm_conv_w, ssm_conv_b, ssm_dt_bias, ssm_a_log, ssm_d,
              ssm_norm_w, ssm_w_out, attn_w_qkv, attn_w_out, final_norm_g):
    c_act = jax.nn.silu(c)
    for i in range(DEPTH):
        h, g = modulate(x, norm_g[i, 0], c_act, mod_w[i, 0], mod_b[i, 0])
        x = x + 0.5 * g * swiglu(h, ffn_w_gate[i, 0], ffn_w_up[i, 0], ffn_w_down[i, 0])
        h, g = modulate(x, norm_g[i, 1], c_act, mod_w[i, 1], mod_b[i, 1])
        j = i // N_MIXERS
        if i % N_MIXERS == 0:
            y = mamba2_mixer(h, ssm_w_in[j], ssm_conv_w[j], ssm_conv_b[j], ssm_dt_bias[j],
                             ssm_a_log[j], ssm_d[j], ssm_norm_w[j], ssm_w_out[j])
        else:
            y = moba_mixer(h, attn_w_qkv[j], attn_w_out[j])
        x = x + g * y
        h, g = modulate(x, norm_g[i, 2], c_act, mod_w[i, 2], mod_b[i, 2])
        x = x + 0.5 * g * swiglu(h, ffn_w_gate[i, 1], ffn_w_up[i, 1], ffn_w_down[i, 1])
    return rmsnorm(x, final_norm_g)


N_A_LAYERS = (DEPTH + 1) // 2
N_B_LAYERS = DEPTH // 2
Q_BLOCK = 128

SB_HEADS = 16
SB_HEAD_DIM = D_MODEL // SB_HEADS

DSA_HEADS = 16
DSA_LATENT = 128
DSA_V_DIM = D_MODEL // DSA_HEADS
IDX_HEADS = 8
IDX_DIM = 64
TOPK_MAX = 256
DSA_IN = DSA_HEADS * DSA_LATENT + DSA_LATENT + IDX_HEADS * IDX_DIM + IDX_DIM + IDX_HEADS

NUM_BUCKETS = 32
MAX_DISTANCE = 128

FFN_DIM = 2816
CONV_W = 3

NEG = -1e30


def rms_norm(x, g):
    xf = x.astype(jnp.float32)
    y = xf * lax.rsqrt(jnp.mean(xf * xf, axis=-1, keepdims=True) + RMS_EPS)
    return (y * g.astype(jnp.float32)).astype(x.dtype)

def _blocks(a):
    B, S = a.shape[0], a.shape[1]
    a = a.reshape((B, S // Q_BLOCK, Q_BLOCK) + a.shape[2:])
    return jnp.moveaxis(a, 1, 0)

def _unblocks(a):
    a = jnp.moveaxis(a, 0, 1)
    return a.reshape((a.shape[0], a.shape[1] * a.shape[2]) + a.shape[3:])

def t5_bucket(dist):
    n = jnp.maximum(dist, 0)
    max_exact = NUM_BUCKETS // 2
    nf = jnp.maximum(n, 1).astype(jnp.float32)
    large = max_exact + (jnp.log(nf / max_exact) / math.log(MAX_DISTANCE / max_exact)
                         * (NUM_BUCKETS - max_exact)).astype(jnp.int32)
    large = jnp.minimum(large, NUM_BUCKETS - 1)
    return jnp.where(n < max_exact, n, large)

def stick_breaking_attention(h, w_in, w_out):
    B, S, _ = h.shape
    qkv = h @ w_in
    q, k, v = jnp.split(qkv, 3, axis=-1)
    q = q.reshape(B, S, SB_HEADS, SB_HEAD_DIM).astype(jnp.float32) * (SB_HEAD_DIM ** -0.5)
    k = k.reshape(B, S, SB_HEADS, SB_HEAD_DIM).astype(jnp.float32)
    v = v.reshape(B, S, SB_HEADS, SB_HEAD_DIM).astype(jnp.float32)
    key_pos = jnp.arange(S)

    def block(args):
        qb, t0 = args
        t = t0 + jnp.arange(Q_BLOCK)
        z = jnp.einsum('bqhd,bshd->bhqs', qb, k)
        strict = key_pos[None, :] < t[:, None]
        log_keep = jnp.where(strict, jax.nn.log_sigmoid(-z), 0.0)
        suffix = lax.cumsum(log_keep, axis=3, reverse=True) - log_keep
        a = jnp.where(strict, jnp.exp(jax.nn.log_sigmoid(z) + suffix), 0.0)
        return jnp.einsum('bhqs,bshd->bqhd', a, v)

    starts = jnp.arange(S // Q_BLOCK) * Q_BLOCK
    o = _unblocks(lax.map(block, (_blocks(q), starts)))
    return o.reshape(B, S, SB_HEADS * SB_HEAD_DIM).astype(h.dtype) @ w_out

def dsa_attention(h, w_in, q_gain, k_gain, w_uv, w_out, rel_bias):
    B, S, _ = h.shape
    topk = min(TOPK_MAX, S // 4)
    proj = h @ w_in
    o1 = DSA_HEADS * DSA_LATENT
    o2 = o1 + DSA_LATENT
    o3 = o2 + IDX_HEADS * IDX_DIM
    o4 = o3 + IDX_DIM
    q, lat, qi, ki, wi = jnp.split(proj, [o1, o2, o3, o4], axis=-1)
    q = rms_norm(q.reshape(B, S, DSA_HEADS, DSA_LATENT), q_gain).astype(jnp.float32)
    k = rms_norm(lat, k_gain).astype(jnp.float32)
    vals = lat.astype(jnp.float32)
    qi = qi.reshape(B, S, IDX_HEADS, IDX_DIM).astype(jnp.float32)
    ki = ki.astype(jnp.float32)
    wi = wi.astype(jnp.float32) * (IDX_HEADS ** -0.5)
    bidx = jnp.arange(B)[:, None, None]
    key_pos = jnp.arange(S)
    scale = DSA_LATENT ** -0.5

    def block(args):
        qb, qib, wib, t0 = args
        t = t0 + jnp.arange(Q_BLOCK)
        isc = jax.nn.relu(jnp.einsum('bqhd,bsd->bqhs', qib, ki))
        isc = jnp.einsum('bqhs,bqh->bqs', isc, wib)
        causal = key_pos[None, :] <= t[:, None]
        isc = jnp.where(causal[None], isc, NEG)
        _, sel = lax.top_k(isc, topk)
        valid = sel <= t[None, :, None]
        kg = k[bidx, sel]
        vg = vals[bidx, sel]
        logits = jnp.einsum('bqhd,bqkd->bqhk', qb, kg) * scale
        bias = rel_bias[t5_bucket(t[None, :, None] - sel)]
        logits = logits + jnp.swapaxes(bias, -1, -2).astype(jnp.float32)
        logits = jnp.where(valid[:, :, None, :], logits, NEG)
        p = jax.nn.softmax(logits, axis=-1)
        return jnp.einsum('bqhk,bqkd->bqhd', p, vg)

    starts = jnp.arange(S // Q_BLOCK) * Q_BLOCK
    o_lat = _unblocks(lax.map(block, (_blocks(q), _blocks(qi), _blocks(wi), starts)))
    o = jnp.einsum('bshl,hlv->bshv', o_lat, w_uv.astype(jnp.float32))
    return o.reshape(B, S, DSA_HEADS * DSA_V_DIM).astype(h.dtype) @ w_out

def conv_ffn(h, w_up, conv_w, conv_b, w_down):
    S = h.shape[1]
    u = h @ w_up
    up = jnp.pad(u, ((0, 0), (CONV_W - 1, 0), (0, 0)))
    y = conv_b
    for j in range(CONV_W):
        y = y + up[:, j:j + S] * conv_w[j]
    gate, val = jnp.split(y, 2, axis=-1)
    return (jax.nn.silu(gate) * val) @ w_down

def second_inputs(seed: int = 0) -> dict:
    key = jax.random.key(seed)
    ks = jax.random.split(key, 20)
    f32 = jnp.float32
    D = D_MODEL

    def nrm(k, shape, s):
        return jax.random.normal(k, shape, f32) * s

    return {
        'x': nrm(ks[0], (BATCH, SEQ, D), 1.0),
        'c': nrm(ks[1], (BATCH, D), 1.0),
        'ada_w': nrm(ks[2], (DEPTH, D, 6 * D), 0.5 * D ** -0.5),
        'ada_b': nrm(ks[3], (DEPTH, 6 * D), 0.01),
        'norm_mix': 1.0 + nrm(ks[4], (DEPTH, D), 0.05),
        'norm_ffn': 1.0 + nrm(ks[5], (DEPTH, D), 0.05),
        'sb_w_in': nrm(ks[6], (N_A_LAYERS, D, 3 * SB_HEADS * SB_HEAD_DIM), D ** -0.5),
        'sb_w_out': nrm(ks[7], (N_A_LAYERS, SB_HEADS * SB_HEAD_DIM, D), (SB_HEADS * SB_HEAD_DIM) ** -0.5),
        'dsa_w_in': nrm(ks[8], (N_B_LAYERS, D, DSA_IN), D ** -0.5),
        'dsa_q_norm': 1.0 + nrm(ks[9], (N_B_LAYERS, DSA_LATENT), 0.05),
        'dsa_k_norm': 1.0 + nrm(ks[10], (N_B_LAYERS, DSA_LATENT), 0.05),
        'dsa_w_uv': nrm(ks[11], (N_B_LAYERS, DSA_HEADS, DSA_LATENT, DSA_V_DIM), DSA_LATENT ** -0.5),
        'dsa_w_out': nrm(ks[12], (N_B_LAYERS, DSA_HEADS * DSA_V_DIM, D), (DSA_HEADS * DSA_V_DIM) ** -0.5),
        'rel_bias': nrm(ks[13], (NUM_BUCKETS, DSA_HEADS), 0.5),
        'ffn_w_up': nrm(ks[14], (DEPTH, D, 2 * FFN_DIM), D ** -0.5),
        'ffn_conv_w': nrm(ks[15], (DEPTH, CONV_W, 2 * FFN_DIM), CONV_W ** -0.5),
        'ffn_conv_b': nrm(ks[16], (DEPTH, 2 * FFN_DIM), 0.01),
        'ffn_w_down': nrm(ks[17], (DEPTH, FFN_DIM, D), FFN_DIM ** -0.5),
    }

def second_block(x, c, ada_w, ada_b, norm_mix, norm_ffn, sb_w_in, sb_w_out, dsa_w_in,
              dsa_q_norm, dsa_k_norm, dsa_w_uv, dsa_w_out, rel_bias, ffn_w_up,
              ffn_conv_w, ffn_conv_b, ffn_w_down):
    cond = jax.nn.silu(c)
    for i in range(DEPTH):
        mod = cond @ ada_w[i] + ada_b[i]
        sh1, sc1, g1, sh2, sc2, g2 = [m[:, None, :] for m in jnp.split(mod, 6, axis=-1)]
        h = rms_norm(x, norm_mix[i]) * (1.0 + sc1) + sh1
        j = i // N_MIXERS
        if i % N_MIXERS == 0:
            mix = stick_breaking_attention(h, sb_w_in[j], sb_w_out[j])
        else:
            mix = dsa_attention(h, dsa_w_in[j], dsa_q_norm[j], dsa_k_norm[j],
                                dsa_w_uv[j], dsa_w_out[j], rel_bias)
        x = x + g1 * mix
        h = rms_norm(x, norm_ffn[i]) * (1.0 + sc2) + sh2
        x = x + g2 * conv_ffn(h, ffn_w_up[i], ffn_conv_w[i], ffn_conv_b[i], ffn_w_down[i])
    return x


def setup_inputs(seed=0):
    out = dict(first_inputs(seed))
    for name, value in second_inputs(seed + 1).items():
        if name != "x":
            out[name + "_2"] = value
    return out


def reference(
    x, c, norm_g, mod_w, mod_b, ffn_w_gate, ffn_w_up, ffn_w_down, ssm_w_in, ssm_conv_w,
    ssm_conv_b, ssm_dt_bias, ssm_a_log, ssm_d, ssm_norm_w, ssm_w_out, attn_w_qkv, attn_w_out,
    final_norm_g, c_2, ada_w_2, ada_b_2, norm_mix_2, norm_ffn_2, sb_w_in_2, sb_w_out_2,
    dsa_w_in_2, dsa_q_norm_2, dsa_k_norm_2, dsa_w_uv_2, dsa_w_out_2, rel_bias_2, ffn_w_up_2,
    ffn_conv_w_2, ffn_conv_b_2, ffn_w_down_2,
):
    x = first_block(
        x, c, norm_g, mod_w, mod_b, ffn_w_gate, ffn_w_up, ffn_w_down, ssm_w_in, ssm_conv_w,
        ssm_conv_b, ssm_dt_bias, ssm_a_log, ssm_d, ssm_norm_w, ssm_w_out, attn_w_qkv,
        attn_w_out, final_norm_g,
    )
    return second_block(
        x, c_2, ada_w_2, ada_b_2, norm_mix_2, norm_ffn_2, sb_w_in_2, sb_w_out_2, dsa_w_in_2,
        dsa_q_norm_2, dsa_k_norm_2, dsa_w_uv_2, dsa_w_out_2, rel_bias_2, ffn_w_up_2,
        ffn_conv_w_2, ffn_conv_b_2, ffn_w_down_2,
    )


_drawn_inputs = setup_inputs


def setup_inputs(seed=0):
    import zlib

    import numpy as np

    out = dict(_drawn_inputs(seed))
    spreads = {}
    factors = {'ssm_conv_b': 6.287,
     'ssm_d': 5.198,
     'ssm_norm_w': 3.286,
     'ada_b_2': 3.425,
     'norm_mix_2': 3.035,
     'norm_ffn_2': 2.69,
     'dsa_q_norm_2': 8.0,
     'dsa_k_norm_2': 8.0,
     'ffn_conv_b_2': 8.0}
    for name, (base, spread) in spreads.items():
        noise = np.random.default_rng([zlib.crc32(name.encode()), seed]).standard_normal(out[name].shape)
        drawn = base * np.exp(spread * noise) if base else spread * noise
        out[name] = __import__('jax').numpy.asarray(drawn.astype(out[name].dtype))
    for name, factor in factors.items():
        out[name] = (out[name] * factor).astype(out[name].dtype)
    return out
```

```python
from contextlib import ExitStack

import numpy as np
import concourse.bass as bass
from concourse import mybir

F32 = mybir.dt.float32
F32R = mybir.dt.float32r
BF16 = mybir.dt.bfloat16
ALU = mybir.AluOpType
ACT = mybir.ActivationFunctionType
AX = mybir.AxisListType

P = 128
T = 256
D = 1024
KT = D // P
DFF = 2816
HD = 64
NFB = DFF // 256
AHEAD = 2
NSLOT = 4
EPS = 1e-6
NEG = -1e30
GONE = -3e38
EXP_LN = "natural_log_exp_and_others"
SILU = "silu_and_others"

STAGES = ["ffn", "mamba", "ffn", "ffn", "moba", "ffn", "sb", "cffn", "dsa", "cffn"]
NJOB = len(STAGES)
RESCALED = 6
GROUP_HEADS = 4
GROUPS = {"ffn": NFB, "cffn": NFB, "mamba": 8, "moba": 4, "sb": 4, "dsa": 4}
NBLK = {"ffn": 3 * NFB, "cffn": 3 * NFB, "mamba": 32, "moba": 16, "sb": 16, "dsa": 15}
RING = {"ffn": 3, "cffn": 3, "mamba": 4, "moba": 4, "sb": 4, "dsa": 3}

PARAM_COLS = [("c", NJOB * 8), ("g", NJOB * 8), ("gfin", 8), ("modb", NJOB * 24), ("wsmall", 8 * 40),
              ("dtb", 32), ("alog", 32), ("cw", 32 * 5), ("dskip", 16), ("ngw", 16), ("fcw", 2 * 44 * 4),
              ("qn", 1), ("kn", 1), ("wuv", 16 * 64), ("relb", 16)]
CONST_COLS = [("ones", P), ("tri", P), ("triL", P), ("ident", P), ("below", P), ("above", P),
              ("dist", 384), ("causal", 384), ("strict", P), ("slope8", 16), ("selmod", 512), ("gmask", 8),
              ("onehot", 384)]


def offsets(cols):
    at, out = 0, {}
    for name, n in cols:
        out[name] = (at, n)
        at += n
    return out, at


PARAMS, NPARAM = offsets(PARAM_COLS)
CONSTS, NCONST = offsets(CONST_COLS)


def constants():
    p = np.arange(P)[:, None]
    c = np.arange(P)[None, :]
    big = np.arange(2 * P)[None, :]
    out = np.zeros((P, NCONST), np.float32)

    def put(name, v):
        at, n = CONSTS[name]
        out[:v.shape[0], at:at + n] = v

    put("ones", np.ones((P, P)))
    put("tri", p <= c)
    put("triL", p >= c)
    put("ident", p == c)
    put("below", np.where(c < p, NEG, 0))
    put("above", np.where(p >= c, -NEG, 0))
    causal = np.concatenate([c <= p, big <= p + P], 1)
    dist = np.concatenate([p - c, p + P - big], 1)
    put("dist", np.where(causal, -dist, NEG))
    put("causal", np.where(causal, 0, NEG))
    put("strict", p < c)
    put("slope8", np.broadcast_to(8.0 * 2.0 ** (-8.0 * (np.arange(16) + 1.0) / 16), (P, 16)))
    k = np.arange(32)[:, None, None]
    put("selmod", np.broadcast_to(k % 4 == np.arange(4)[None, :, None], (32, 4, P)).reshape(32, 512))
    put("gmask", np.arange(32)[:, None] // 4 == np.arange(8)[None, :])
    n = np.maximum(255 - np.arange(384), 0)
    nf = np.maximum(n, 1).astype(np.float32)
    large = 16 + (np.log(nf / np.float32(16)) / np.float32(np.log(8.0)) * np.float32(16)).astype(np.int32)
    bucket = np.where(n < 16, n, np.minimum(large, 31))
    put("onehot", np.arange(32)[:, None] == bucket[None, :])
    return out


class Plan:

    def __init__(self, stages):
        self.stages = stages
        self.first = []
        self.slot, self.use = [], []
        used = [0] * NSLOT
        for kind in stages:
            self.first.append(len(self.slot))
            for n in range(NBLK[kind]):
                s = n % RING[kind]
                self.slot.append(s)
                self.use.append(used[s])
                used[s] += 1
        self.nblk = len(self.slot)
        self.base, self.tally = {}, {}
        total = {}
        for st, kind in enumerate(stages):
            for name, n in self.steps(st, kind).items():
                self.base.setdefault(name, {})[st] = total.get(name, 0)
                total[name] = total.get(name, 0) + n
            for name in total:
                self.base[name].setdefault(st, total[name])
        for name in total:
            for st in range(len(stages)):
                self.base[name].setdefault(st, 0)
            self.base[name][len(stages)] = total[name]
        self.total = total

    def steps(self, st, kind):
        g = GROUPS[kind]
        out = {"mods": 1, "modv": 1, "xup": 8, "sq": 8, "ss": 1, "ln": 1, "rstd": 1, "t": 8, "hhi": 8,
               "hlo": 8, "zero": 1, "ahi": 0, "alo": 0}
        if st == RESCALED:
            out |= {"sq": 16, "ss": 2, "ln": 2, "rstd": 2, "xfin": 8}
        if kind in ("ffn", "cffn"):
            out |= {"silu": g, "mul": g, "ahi": g, "alo": g}
        if kind == "cffn":
            out |= {"cid": 2 * g, "tap1": 2 * g, "tap2": 2 * g}
        if kind == "mamba":
            out |= {"dtp": 1, "dta": 11, "dtx": 4, "acp": 1, "acv": 2, "sq0": 1, "cid": 2 * g, "tap": 6 * g,
                    "sil": 3 * g, "acg": g, "xt": g, "cb": g, "br": 4 * g, "xdt": g, "cbs": g, "dx": g,
                    "dec": 4 * g, "wv": 4 * g, "yc": g, "y1": g, "yz": g, "ysq": g, "yn": g, "yac": g,
                    "ahi": g, "alo": g, "rs2p": 1, "rs2": 2, "xr": 8}
        if kind in ("moba", "sb", "dsa"):
            out |= {"sc": 4 * g, "qev": g, "lg": 4 * g, "ptp": 4 * g, "ptc": 4 * g, "pv": 2 * g,
                    "ahi": 2 * g, "alo": 2 * g}
        if kind in ("moba", "sb"):
            out |= {"kev": g, "vev": g}
        if kind in ("moba", "dsa"):
            out |= {"mx": 4 * g, "nm": 4 * g, "ex": 4 * g, "rc": 4 * g, "prb": 4 * g}
        if kind == "sb":
            out |= {"ab": 4 * g, "ea": 4 * g, "la": 4 * g, "lk": 4 * g, "prb": 4 * g, "arg": 4 * g}
        if kind == "dsa":
            out |= {"qev2": g, "pre": 3, "wip": 1, "relp": 1, "wiv": 1, "relv": 1, "ix": 8, "rel": 8,
                    "isc": 10, "top": 32, "msk": 2, "ksq": 1, "kss": 1, "klr": 2, "gkq": 1, "kn": 1,
                    "ltp": 1, "ltc": 1, "qsq": 2 * g, "qss": g, "qlr": 2 * g, "ol": 2 * g, "olc": 2 * g, "wu": g}
        return out


class Steps:

    def __init__(self, eng, plan, sems):
        self.eng, self.plan, self.sems = eng, plan, sems
        self.trips = 1

    def loop(self, a, b):
        self.trips = b - a
        with self.eng.Fori(a, b) as i:
            yield i
        self.trips = 1

    def inc(self, name, ins):
        ins.then_inc(self.sems[name], 1)
        self.plan.tally[name] = self.plan.tally.get(name, 0) + self.trips
        return ins

    def wait(self, name, st, i=0, a=0, b=0):
        v = self.plan.base[name][st] + b + 1
        v = i * a + v if a else v
        if isinstance(v, int) and v <= 0:
            return
        self.eng.wait_ge(self.sems[name], v)

    def block(self, st, i=0, a=0, b=0, it=None):
        plan, at = self.plan, self.plan.first[st] + b
        if it is None:
            g = at + i * a
            if g >= plan.nblk:
                return None
            return g, plan.slot[g], plan.use[g]
        g0 = at + it[0] * a
        for n in range(*it):
            g = at + n * a
            assert plan.slot[g] == plan.slot[g0] and plan.use[g] == plan.use[g0] + n - it[0]
        return i * a + at, plan.slot[g0], i + (plan.use[g0] - it[0])


def build(nc, weights, mods, params, consts, xin, out, stages=None):
    stages = stages or STAGES
    plan = Plan(stages)
    NST = len(stages)
    with ExitStack() as ctx:
        def sb(name, shape, dt=F32):
            return ctx.enter_context(nc.sbuf_tensor(name, shape, dt))

        raw = [sb(f"raw{s}", [P, 2048]) for s in range(NSLOT)]
        w_hi = [sb(f"w_hi{s}", [P, 2048], F32R) for s in range(NSLOT)]
        w_lo = [sb(f"w_lo{s}", [P, 2048], F32R) for s in range(NSLOT)]
        x = sb("x", [P, KT, T])
        h_hi = sb("h_hi", [P, KT, T], F32R)
        h_lo = sb("h_lo", [P, KT, T], F32R)
        work = sb("work", [P, KT * T])
        work3 = work[:, :].rearrange("p (k t) -> p k t", k=KT)
        modws = sb("modws", [P, 3072])
        modw = [modws[:, 1536 * s:1536 * (s + 1)] for s in range(2)]
        macc = sb("macc", [P, 3072])
        modv = sb("modv", [P, NJOB, 24])
        gs = sb("gs", [P, NJOB, 8])
        par = sb("par", [P, NPARAM])
        con = sb("con", [P, NCONST])
        conb = sb("conb", [P, 3 * P + 896], BF16)
        ws_hi = sb("ws_hi", [P, 8 * 40], F32R)
        ws_lo = sb("ws_lo", [P, 8 * 40], F32R)
        small = sb("small", [P, 64])
        cact = sb("cact", [P, NJOB * 8])
        cj = sb("cj", [P, 8])[:, :]
        rstd = sb("rstd", [P, T])
        a_hi = sb("a_hi", [P, 2, T], F32R)
        a_lo = sb("a_lo", [P, 2, T], F32R)
        mix = sb("mix", [P, 6144])
        first_mod = [mix[:, 0:3072], mix[:, 3072:6144], modws[:, :]]
        bank = [ctx.enter_context(nc.psum_tensor(f"bank{n}", [P, 512], F32)) for n in range(8)]
        scratch = nc.dram_tensor("scratch", (16, 384), F32, kind="Internal").ap()
        biases = nc.dram_tensor("biases", (P, 16, T), F32, kind="Internal").ap()

        def sem(name):
            return ctx.enter_context(nc.semaphore("s_" + name))

        sems = {n: sem(n) for n in list(plan.total) + ["blk", "whi", "wlo", "macc", "const", "cact", "xst", "mo"]}
        s_raw = [sem(f"raw{s}") for s in range(NSLOT)]
        s_mo = [sem(f"mo{s}") for s in range(3)]
        s_modw = [sem(f"modw{s}") for s in range(2)]
        s_in, s_par, s_con, s_out, s_rel, s_bias = (sem(n) for n in ("in", "par", "con", "out", "relst", "bias"))

        def view(off, *dims):
            n = int(np.prod(dims))
            v = mix[:, off:off + n]
            if len(dims) == 2:
                v = v.rearrange("p (a b) -> p a b", a=dims[0])
            if len(dims) == 3:
                v = v.rearrange("p (a b c) -> p a b c", a=dims[0], b=dims[1])
            return v

        def par_(name, at=0, n=None):
            o, w = PARAMS[name]
            if isinstance(at, int):
                return par[:, o + at:o + at + (w if n is None else n)]
            return par[:, bass.ds(at + o, n)]

        def con_(name, rows=P):
            o, w = CONSTS[name]
            return con[0:rows, o:o + w]

        ident_b, below_b, above_b = conb[:, 0:P], conb[:, P:2 * P], conb[:, 2 * P:3 * P]
        zero_b = conb[:, 3 * P:3 * P + 512]
        eps_c, eps128_c, one_c = small[:, 0:1], small[:, 1:2], small[:, 2:3]

        def acc(m):
            return bank[m // 2][:, (m % 2) * T:(m % 2 + 1) * T]

        sg = view(0, 2, T)
        act = view(512, 2, T)
        cg = view(1024, 2, T)
        cu = view(1536, 2, T)
        xc, bc, zc, dx = (view(512 * n, 2, T) for n in range(4))
        xdt = view(2048, 2, T)
        cbs = mix[:, 2560:2944]
        acg = mix[0:32, 2944:3328]
        yb = view(3328, 2, T)
        sqa = view(3840, 2, T)
        sqt = view(4352, 2, T)
        acT = mix[0:32, 4864:5248]
        dtt, dta, nac, dv, de, dw, dl, dm = (mix[:, 5248 + 64 * n:5312 + 64 * n] for n in range(8))
        ea = mix[:, 5760:5792]
        r2 = mix[:, 5792:6048]
        yn = work[:, 1536:2048].rearrange("p (a t) -> p a t", a=2)
        Q = view(0, 4, T)
        KB = view(1024, 2, T)
        VB = view(1536, 2, T)
        PT = view(2048, 2, 384)
        mxt, nmx, sums, rcp = (mix[:, 2816 + 8 * n:2824 + 8 * n] for n in range(4))
        S = work[:, 0:1536].rearrange("p (h c) -> p h c", h=4)
        LK = view(3072, 4, 384)
        kn, ltok = mix[:, 1024:1280], view(1280, 2, P)
        wu = mix[:, 1536:1792]
        rq = mix[:, 1792:1800]
        wi = view(1800, 2, 8)
        gkq = mix[:, 1816:1817]
        v8 = mix[:, 1824:1832]
        OL = view(3072, 2, T)
        bias = view(3584, 4, T)
        maskb = conb[:, 3 * P + 512:3 * P + 896]
        latT, ki2 = mix[:, 2048:2304], mix[:, 3072:3328]
        R = view(4608, 2, 384)
        isc, wk = mix[:, 5376:5760], mix[:, 5760:6144]
        relS = mix[0:16, 3584:3968]
        qsq = [work[:, 1536:2048], mix[:, 3072:3584]]

        block = ctx.enter_context(nc.Block())

        @block.sync
        def _(eng):
            k = Steps(eng, plan, sems)
            for n in range(KT):
                if n >= 3:
                    eng.wait_ge(sems["mo"], n - 2)
                eng.dma_start(first_mod[n % 3], mods[n]).then_inc(s_mo[n % 3], 16)
                if n == 2:
                    eng.dma_start(con[:, :], consts).then_inc(s_con, 16)
                    eng.dma_start(x[:, :, :], xin).then_inc(s_in, 16)

            def load(st, i, a, b, it=None, wait=True):
                g, s, _ = k.block(st, i, a, b, it)
                if wait:
                    eng.wait_ge(sems["wlo"], g - 2)
                src = weights[g] if it is None else weights[bass.ds(g, 1)].rearrange("a p n -> (a p) n")
                eng.dma_start(raw[s][:, :], src).then_inc(s_raw[s], 16)

            for st, kind in enumerate(stages):
                ring, n = RING[kind], NBLK[kind]
                a = 0
                if st == 0:
                    for b in range(ring):
                        load(st, 0, 0, b, wait=b >= 3)
                    a = 1
                for i in k.loop(a, n // ring):
                    for b in range(ring):
                        load(st, i, ring, b, (a, n // ring))
            for m in range(KT):
                eng.wait_ge(sems["xup"], plan.base["xup"][NST - 1] + m + 1)
                eng.dma_start(out[:, m, :], x[:, m, :]).then_inc(s_out, 16)
            eng.wait_ge(s_out, 16 * KT)

        @block.gpsimd
        def _(eng):
            k = Steps(eng, plan, sems)

            def load(q, half):
                src = mods[q] if isinstance(q, int) else mods[bass.ds(q, 1)].rearrange("a p n -> (a p) n")
                eng.dma_start(modw[half], src[:, half * 1536:(half + 1) * 1536]).then_inc(s_modw[half], 16)

            per = 1 + 2 + 4 * 7

            def job(j, last=False):
                j1, at = j - 1, 1

                def step(ins):
                    nonlocal at
                    ins.then_inc(sems["macc"], 1)
                    eng.wait_ge(sems["macc"], j1 * per + at)
                    at += 1

                src = cact[:, 8 * j:8 * j + 8] if isinstance(j, int) else cact[:, bass.ds(j * 8, 8)]
                step(eng.tensor_copy(cj, src))
                for n in range(8):
                    for half in range(2):
                        eng.wait_ge(s_modw[half], j1 * 128 + (n + 1) * 16)
                        w, m = modw[half], macc[:, half * 1536:(half + 1) * 1536]
                        c = cj[:, n:n + 1].to_broadcast([P, 1536])
                        if n == 0:
                            if half == 0:
                                eng.wait_ge(sems["mods"], j)
                            step(eng.tensor_tensor(m, w, c, ALU.mult))
                        else:
                            step(eng.tensor_tensor(w, w, c, ALU.mult))
                            step(eng.tensor_tensor(m, m, w, ALU.add))
                        if not (last and n == 7):
                            load(j * 8 + (n + 1), half)

            if NST > 1:
                eng.wait_ge(sems["mo"], 8)
                eng.wait_ge(sems["cact"], 1)
                load(8, 0)
                load(8, 1)
                if NST > 2:
                    for j in k.loop(1, NST - 1):
                        job(j)
                job(NST - 1, True)

        @block.scalar
        def _(eng):
            k = Steps(eng, plan, sems)
            eng.dma_start(par[:, :], params).then_inc(s_par, 16)
            eng.wait_ge(s_par, 16)
            k.inc("cact", eng.activation(cact[:, :], par_("c"), ACT.Silu))
            eng.wait_ge(s_con, 16)
            for n, name in enumerate(("ident", "below", "above")):
                eng.activation(conb[:, n * P:(n + 1) * P], con_(name), ACT.Copy)
            eng.activation(ws_hi[:, :], par_("wsmall"), ACT.Copy).then_inc(sems["const"], 1)

            def split(st, i=0, a=0, b=0, it=None):
                blk = k.block(st, i, a, b + AHEAD, it)
                if blk is None:
                    return
                g, s, use = blk
                eng.wait_ge(s_raw[s], use * 16 + 16)
                if it is not None or g >= 3:
                    eng.wait_ge(sems["blk"], g - 2)
                eng.activation(w_hi[s][:, :], raw[s][:, :], ACT.Copy).then_inc(sems["whi"], 1)

            def rs(out_, in_, scale, eps, name, st, i=0, a=0, b=0):
                k.inc(name[0], eng.activation(out_, in_, ACT.Ln, bias=eps, scale=scale))
                k.wait(name[0], st, i, a, b)
                return k.inc(name[1], eng.activation(out_, out_, ACT.Exp, scale=-0.5))

            def norm(st):
                eng.preload_act_table_set(EXP_LN)
                for rnd in range(2 if st == RESCALED else 1):
                    for m in range(KT):
                        if rnd == 1:
                            k.wait("xfin", st, b=m)
                        elif st:
                            k.wait("xup", st - 1, b=m)
                        elif m == 0:
                            eng.wait_ge(s_in, 16)
                        k.inc("sq", eng.activation(work3[:, m, :], x[:, m, :], ACT.Square))
                    k.wait("ss", st, b=rnd)
                    rs(rstd[:, :], bank[6][:, 0:T], 1.0 / D, eps_c, ("ln", "rstd"), st, b=rnd)
                for m in range(KT):
                    k.wait("t", st, b=m)
                    k.inc("hhi", eng.activation(h_hi[:, m, :], work3[:, m, :], ACT.Identity,
                                                bias=modv[:, st, m:m + 1]))

            def ffn(st):
                def gate(i, a, b, loop):
                    split(st, i, a, b, loop)
                    eng.wait_ge(sems["blk"], k.block(st, i, a, b, loop)[0] + 1)
                    k.wait("mul", st, i, 1, -1)
                    k.inc("silu", eng.activation(sg, bank[4][:, :].rearrange("p (a t) -> p a t", a=2), ACT.Silu))

                def up(i, a, b, loop):
                    split(st, i, a, b, loop)

                def down(i, a, b, loop):
                    split(st, i, a, b, loop)
                    hi(i, a, b, loop)

                def hi(i, a, b, loop):
                    if a or b:
                        eng.wait_ge(sems["blk"], k.block(st, i, a, b, loop)[0] + 1)
                    k.wait("mul", st, i, 1, 0)
                    k.inc("ahi", eng.activation(a_hi[:, :, :], act, ACT.Copy))

                gate(0, 0, 0, None)
                up(0, 0, 1, None)
                hi(0, 0, 0, None)
                for i in k.loop(1, NFB - 1):
                    r = (1, NFB - 1)
                    gate(i, 3, -1, r)
                    up(i, 3, 0, r)
                    down(i, 3, 1, r)
                n = NFB - 1
                gate(n, 3, -1, None)
                up(n, 3, 0, None)
                down(n, 3, 1, None)
                split(st, 0, 0, 3 * n + 2)

            def cffn(st):
                ci = sum(1 for z in stages[:st] if z == "cffn")

                def cw(i, tile, tap):
                    if isinstance(i, int):
                        return par_("fcw", ((ci * 44 + 2 * i + tile) * 4) + tap, 1)
                    return par_("fcw", i * 8 + (ci * 44 + tile) * 4 + tap, 1)

                def taps(i, up):
                    b, dst = bank[5 if up else 4], cu if up else cg
                    k.wait("mul", st, i, 1, -1)
                    for m in range(2):
                        t = 22 * up + m
                        ins = eng.activation(dst[:, m, :], b[:, m * T:(m + 1) * T], ACT.Identity,
                                             scale=cw(i, t, 2), bias=cw(i, t, 3))
                    k.inc("cid", ins)

                def gate(i, a, b, loop):
                    split(st, i, a, b, loop)
                    eng.wait_ge(sems["blk"], k.block(st, i, a, b, loop)[0] + 1)
                    taps(i, 0)

                def up(i, a, b, loop):
                    split(st, i, a, b, loop)
                    k.wait("tap2", st, i, 2, 0)
                    k.inc("silu", eng.activation(sg, cg, ACT.Silu))
                    eng.wait_ge(sems["blk"], k.block(st, i, a, b, loop)[0] + 1)
                    taps(i, 1)

                def hi(i, a, b, loop):
                    if a or b:
                        eng.wait_ge(sems["blk"], k.block(st, i, a, b, loop)[0] + 1)
                    k.wait("mul", st, i, 1, 0)
                    k.inc("ahi", eng.activation(a_hi[:, :, :], act, ACT.Copy))

                def down(i, a, b, loop):
                    split(st, i, a, b, loop)
                    hi(i, a, b, loop)

                gate(0, 0, 0, None)
                up(0, 0, 1, None)
                hi(0, 0, 0, None)
                for i in k.loop(1, NFB - 1):
                    r = (1, NFB - 1)
                    gate(i, 3, -1, r)
                    up(i, 3, 0, r)
                    down(i, 3, 1, r)
                n = NFB - 1
                gate(n, 3, -1, None)
                up(n, 3, 0, None)
                down(n, 3, 1, None)
                split(st, 0, 0, 3 * n + 2)

            def done(st, i, a, b, loop):
                eng.wait_ge(sems["blk"], k.block(st, i, a, b, loop)[0] + 1)

            def mamba(st):
                k.wait("dta", st, b=0)
                k.inc("dtx", eng.activation(de, dv, ACT.Abs))
                k.wait("dtx", st, b=0)
                k.inc("dtx", eng.activation(de, de, ACT.Exp, scale=-1.0))
                k.wait("dta", st, b=1)
                k.inc("dtx", eng.activation(dl, dw, ACT.Ln))
                k.inc("dtx", eng.activation(ea, par_("alog"), ACT.Exp))

                def conv(i, dst, b, first, free):
                    free()
                    for m in range(2):
                        t = first + m
                        sc, bi = (par_("cw", i * 20 + 5 * t + tap, 1) for tap in (3, 4))
                        ins = eng.activation(dst[:, m, :], b[:, m * T:(m + 1) * T], ACT.Identity, scale=sc, bias=bi)
                    k.inc("cid", ins)

                def silu(i, n, dst, src):
                    k.inc("sil", eng.activation(dst, src, ACT.Silu))

                def decay(i, off, h):
                    k.wait("br", st, i, 4, 4 * off + h)
                    if h == 0:
                        k.wait("yc", st, i, 1, off - 1)
                    b = bank[6 + h % 2]
                    for c0, c1, tt in ((0, 256, 0), (256, 384, 1)):
                        at = i * 4 + (4 * off + h)
                        nb = nac[:, 32 * tt + at:32 * tt + at + 1] if isinstance(at, int) else \
                            nac[:, bass.ds(at + 32 * tt, 1)]
                        ins = eng.activation(S[:, h, c0:c1], b[:, c0:c1], ACT.Exp, bias=nb)
                    k.inc("dec", ins)

                def body(i, loop, a, b):
                    more = not isinstance(i, int) or i > 0
                    split(st, i, a, b, loop)
                    done(st, i, a, b, loop)
                    conv(i, xc, bank[4], 0, lambda: (k.wait("xt", st, i, 1, -1), k.wait("dx", st, i, 1, -1)))
                    if more:
                        decay(i, -1, 2)
                        decay(i, -1, 3)
                    split(st, i, a, b + 1, loop)
                    k.wait("tap", st, i, 6, 2)
                    silu(i, 0, xc, xc)
                    done(st, i, a, b + 1, loop)
                    conv(i, bc, bank[5], 2, lambda: k.wait("cb", st, i, 1, -1))
                    split(st, i, a, b + 2, loop)
                    k.wait("tap", st, i, 6, 5)
                    silu(i, 1, bc, bc)
                    if more:
                        y_parts(i)
                    done(st, i, a, b + 2, loop)
                    k.wait("yz", st, i, 1, -1)
                    silu(i, 2, zc, bank[7][:, :].rearrange("p (a t) -> p a t", a=2))
                    if more:
                        split(st, i, a, b + 3, loop)
                    decay(i, 0, 0)
                    decay(i, 0, 1)

                def y_parts(i):
                    k.wait("yz", st, i, 1, -1)
                    k.wait("yac", st, i, 1, -2)
                    k.inc("ysq", eng.activation(sqt, yb, ACT.Square))
                    k.wait("yn", st, i, 1, -1)
                    k.inc("ahi", eng.activation(a_hi[:, :, :], yn, ACT.Copy))

                n = GROUPS["mamba"]
                body(0, None, 0, 0)
                for i in k.loop(1, n):
                    body(i, (1, n), 4, -1)
                decay(n, -1, 2)
                decay(n, -1, 3)
                y_parts(n)
                eng.preload_act_table_set(EXP_LN)
                split(st, 0, 0, 4 * n - 1)
                k.wait("rs2p", st)
                rs(r2, bank[6][:, 0:T], 1.0 / 2048, eps_c, ("rs2", "rs2"), st)

            def heads(st, kind):
                n = GROUPS[kind]
                scale = 0.125 if kind == "moba" else 1.0

                def softmax(i, h):
                    if kind == "sb":
                        if h == 0:
                            k.wait("ptp", st, i, 4, -1)
                        k.wait("lg", st, i, 4, h)
                        k.inc("ab", eng.activation(LK[:, h, :], S[:, h, :], ACT.Abs))
                        k.wait("ab", st, i, 4, h)
                        k.inc("ea", eng.activation(LK[:, h, :], LK[:, h, :], ACT.Exp, scale=-1.0))
                        k.wait("ea", st, i, 4, h)
                        k.inc("la", eng.activation(LK[:, h, :], LK[:, h, :], ACT.Ln, bias=one_c))
                        return
                    k.wait("nm", st, i, 4, h)
                    for c0, c1, tt in ((0, 128, 0), (128, 384, 1)):
                        ins = eng.activation(S[:, h, c0:c1], S[:, h, c0:c1], ACT.Exp, scale=scale,
                                             bias=nmx[:, 2 * h + tt:2 * h + tt + 1],
                                             accum_out=sums[:, 2 * h + tt:2 * h + tt + 1])
                    k.inc("ex", ins)

                def pt(i, h):
                    if h % 2 == 0:
                        k.wait("pv", st, i, 2, -2 + h // 2 - 1)
                    if kind == "sb":
                        k.wait("arg", st, i, 4, h - 4)
                        k.inc("ptc", eng.activation(PT[:, h % 2, :], S[:, h, :], ACT.Exp))
                    else:
                        k.wait("ptp", st, i, 4, h - 4)
                        k.inc("ptc", eng.activation(PT[:, h % 2, :], bank[7 - h % 2][:, 0:384], ACT.Copy))

                def out_hi(i, p, loop):
                    if kind == "dsa":
                        k.wait("olc", st, i, 2, p - 2)
                    else:
                        k.wait("pv", st, i, 2, p - 2)
                    b = bank[5 if kind == "dsa" else 4]
                    k.inc("ahi", eng.activation(a_hi[:, p, :], b[:, p * T:(p + 1) * T], ACT.Copy))

                def latent(i, p):
                    k.wait("pv", st, i, 2, p - 2)
                    k.wait("olc", st, i, 2, p - 3)
                    k.inc("ol", eng.activation(OL, bank[4][:, :].rearrange("p (a t) -> p a t", a=2), ACT.Copy))

                def evac(name, dst, b, sc=1.0):
                    return k.inc(name, eng.activation(dst, b[:, :].rearrange("p (a t) -> p a t", a=2), ACT.Copy,
                                                      scale=sc))

                def load_bias(i):
                    if not isinstance(i, int) or i > 0:
                        k.wait("lg", st, i, 4, -1)
                    src = biases[:, 0:4, :] if isinstance(i, int) else biases[:, bass.ds(i * 4, 4), :]
                    eng.dma_start(bias, src).then_inc(s_bias, 16)

                def body(i, loop, a, b, more):
                    split(st, i, a, b, loop)
                    done(st, i, a, b, loop)
                    if more:
                        k.wait("sc", st, i, 4, -1)
                    evac("qev", Q[:, 0:2, :], bank[4], 0.125 if kind == "sb" else 1.0)
                    if kind == "dsa":
                        k.wait("qev", st, i, 1, 0)
                        k.inc("qsq", eng.activation(qsq[0], mix[:, 0:512], ACT.Square))
                    split(st, i, a, b + 1, loop)
                    if more:
                        pt(i, 0)
                        pt(i, 1)
                    done(st, i, a, b + 1, loop)
                    if kind == "dsa":
                        evac("qev2", Q[:, 2:4, :], bank[5])
                        if more:
                            latent(i, 0)
                            pt(i, 2)
                            pt(i, 3)
                            out_hi(i, 0, loop)
                            latent(i, 1)
                            out_hi(i, 1, loop)
                            split(st, i, a, b + 2, loop)
                            k.wait("olc", st, i, 2, -1)
                        k.wait("qev2", st, i, 1, 0)
                        k.inc("qsq", eng.activation(qsq[1], mix[:, 512:1024], ACT.Square))
                        k.inc("wu", eng.activation(wu, par_("wuv", i * 256, 256), ACT.Copy))
                        k.wait("qss", st, i, 1, 0)
                        rs(rq, bank[7][:, 0:8], 1.0, eps128_c, ("qlr", "qlr"), st, i, 2, 0)
                    else:
                        evac("kev", KB, bank[5])
                        split(st, i, a, b + 2, loop)
                        if more:
                            out_hi(i, 0, loop)
                            pt(i, 2)
                            pt(i, 3)
                            out_hi(i, 1, loop)
                        done(st, i, a, b + 2, loop)
                        evac("vev", VB, bank[5])
                        if more:
                            split(st, i, a, b + 3, loop)
                    for h in range(4):
                        softmax(i, h)

                if kind == "dsa":
                    sparse_front(st)
                    load_bias(0)
                    body(0, None, 0, 3, False)
                    for i in k.loop(1, n):
                        load_bias(i)
                        body(i, (1, n), 3, 2, True)
                else:
                    body(0, None, 0, 0, False)
                    for i in k.loop(1, n):
                        body(i, (1, n), 4, -1, True)
                pt(n, 0)
                pt(n, 1)
                if kind == "dsa":
                    latent(n, 0)
                    pt(n, 2)
                    pt(n, 3)
                    out_hi(n, 0, None)
                    latent(n, 1)
                    out_hi(n, 1, None)
                else:
                    out_hi(n, 0, None)
                    pt(n, 2)
                    pt(n, 3)
                    out_hi(n, 1, None)
                split(st, 0, 0, NBLK[kind] - 1)

            def sparse_front(st):
                k.wait("relv", st)
                eng.dma_start(scratch, relS).then_inc(s_rel, 16)
                two = dict(a=2)
                eng.wait_ge(s_rel, 16)
                eng.dma_start(biases.rearrange("p h c -> h p c"),
                              bass.AP(scratch.tensor, 127, [[384, 16], [-1, P], [1, T]])).then_inc(s_rel, 16)
                split(st, b=0)
                done(st, 0, 0, 0, None)
                eng.activation(latT, bank[4][:, 0:T], ACT.Copy)
                k.inc("pre", eng.activation(ki2, bank[4][:, T:2 * T], ACT.Copy))
                k.wait("pre", st, b=0)
                k.inc("ksq", eng.activation(qsq[0][:, 0:T], latT, ACT.Square))
                split(st, b=1)
                done(st, 0, 0, 1, None)
                k.inc("pre", eng.activation(Q[:, 0:2, :], bank[5][:, :].rearrange("p (a t) -> p a t", **two), ACT.Copy))
                k.wait("kss", st)
                rs(rstd[:, :], bank[7][:, 0:T], 1.0 / P, eps_c, ("klr", "klr"), st)
                split(st, b=2)
                done(st, 0, 0, 2, None)
                k.inc("pre", eng.activation(Q[:, 2:4, :], bank[6][:, :].rearrange("p (a t) -> p a t", **two), ACT.Copy))
                for h in range(8):
                    k.wait("ix", st, b=h)
                    if h >= 2:
                        k.wait("isc", st, b=h - 1)
                    k.inc("rel", eng.activation(R[:, h % 2, :], bank[4 + h % 2][:, 0:384], ACT.Relu))
                k.wait("ltp", st)
                k.inc("ltc", eng.activation(ltok, bank[7][:, 0:T].rearrange("p (a t) -> p a t", **two), ACT.Copy))
                eng.wait_ge(s_rel, 32)

            programs = {"ffn": ffn, "cffn": cffn, "mamba": mamba, "moba": lambda st: heads(st, "moba"),
                        "sb": lambda st: heads(st, "sb"), "dsa": lambda st: heads(st, "dsa")}
            for b in range(-AHEAD, 0):
                split(0, b=b)
            for st, kind in enumerate(stages):
                norm(st)
                if kind in ("ffn", "cffn"):
                    eng.preload_act_table_set(SILU)
                programs[kind](st)

        @block.vector
        def _(eng):
            k = Steps(eng, plan, sems)
            eng.memset(eps_c, EPS)
            eng.memset(eps128_c, EPS * P)
            eng.memset(one_c, 1.0)
            eng.memset(zero_b, 0.0).then_inc(sems["xst"], 1)
            eng.wait_ge(sems["const"], 1)
            eng.tensor_tensor(ws_lo[:, :], par_("wsmall"), ws_hi[:, :], ALU.subtract).then_inc(sems["xst"], 1)

            def split(st, i=0, a=0, b=0, it=None):
                blk = k.block(st, i, a, b + AHEAD, it)
                if blk is None:
                    return
                g, s, _ = blk
                eng.wait_ge(sems["whi"], g + 1)
                eng.tensor_tensor(w_lo[s][:, :], raw[s][:, :], w_hi[s][:, :], ALU.subtract).then_inc(sems["wlo"], 1)

            def modulation(st):
                k.wait("mods", st)
                mv = modv[:, st, :]
                ins = eng.tensor_tensor(mv, bank[7][:, 0:24], par_("modb", 24 * st, 24), ALU.add)
                ins.then_inc(sems["xst"], 1)
                eng.wait_ge(sems["xst"], 2 + 2 * st + 1)
                if stages[st] == "ffn":
                    eng.tensor_scalar(mv[:, 16:24], mv[:, 16:24], 0.5, None, ALU.mult)
                eng.tensor_scalar(gs[:, st, :], mv[:, 8:16], 1.0, None, ALU.add).then_inc(sems["xst"], 1)
                eng.wait_ge(sems["xst"], 2 + 2 * st + 2)
                k.inc("modv", eng.tensor_tensor(gs[:, st, :], gs[:, st, :], par_("g", 8 * st, 8), ALU.mult))

            def norm(st):
                if st == RESCALED:
                    k.wait("rstd", st, b=0)
                    for m in range(KT):
                        k.inc("xfin", eng.scalar_tensor_tensor(
                            out=x[:, m, :], in0=x[:, m, :], scalar=par_("gfin", m, 1), in1=rstd[:, :],
                            op0=ALU.mult, op1=ALU.mult))
                k.wait("rstd", st, b=1 if st == RESCALED else 0)
                k.wait("modv", st)

                def low(m):
                    k.wait("hhi", st, b=m)
                    k.inc("hlo", eng.scalar_tensor_tensor(
                        out=h_lo[:, m, :], in0=work3[:, m, :], scalar=modv[:, st, m:m + 1],
                        in1=h_hi[:, m, :], op0=ALU.add, op1=ALU.subtract))

                for m in range(KT):
                    k.inc("t", eng.scalar_tensor_tensor(
                        out=work3[:, m, :], in0=x[:, m, :], scalar=gs[:, st, m:m + 1], in1=rstd[:, :],
                        op0=ALU.mult, op1=ALU.mult))
                    if m:
                        low(m - 1)
                low(KT - 1)

            def residual(st):
                eng.wait_ge(sems["blk"], plan.first[st] + NBLK[stages[st]])
                if stages[st] == "mamba":
                    k.wait("rs2", st, b=1)
                    for m in range(KT):
                        k.inc("xr", eng.tensor_tensor(work3[:, m, :], acc(m), r2, ALU.mult))
                for m in range(KT):
                    if stages[st] == "mamba":
                        k.wait("xr", st, b=m)
                        k.inc("xup", eng.scalar_tensor_tensor(
                            out=x[:, m, :], in0=work3[:, m, :], scalar=modv[:, st, 16 + m:17 + m],
                            in1=x[:, m, :], op0=ALU.mult, op1=ALU.add))
                        continue
                    k.inc("xup", eng.scalar_tensor_tensor(
                        out=x[:, m, :], in0=acc(m), scalar=modv[:, st, 16 + m:17 + m], in1=x[:, m, :],
                        op0=ALU.mult, op1=ALU.add))

            def ffn(st):
                def gate(i, a, b, loop):
                    split(st, i, a, b, loop)

                def up(i, a, b, loop):
                    split(st, i, a, b, loop)
                    eng.wait_ge(sems["blk"], k.block(st, i, a, b, loop)[0] + 1)
                    k.wait("silu", st, i, 1, 0)
                    k.wait("alo", st, i, 1, -1)
                    k.inc("mul", eng.tensor_tensor(act, sg, bank[5][:, :].rearrange("p (a t) -> p a t", a=2),
                                                   ALU.mult))

                def lo(i):
                    k.wait("ahi", st, i, 1, 0)
                    k.inc("alo", eng.tensor_tensor(a_lo[:, :, :], act, a_hi[:, :, :], ALU.subtract))

                def down(i, a, b, loop):
                    split(st, i, a, b, loop)
                    lo(i)

                gate(0, 0, 0, None)
                up(0, 0, 1, None)
                lo(0)
                for i in k.loop(1, NFB - 1):
                    r = (1, NFB - 1)
                    gate(i, 3, -1, r)
                    up(i, 3, 0, r)
                    down(i, 3, 1, r)
                n = NFB - 1
                gate(n, 3, -1, None)
                up(n, 3, 0, None)
                down(n, 3, 1, None)
                split(st, 0, 0, 3 * n + 2)

            def cffn(st):
                ci = sum(1 for z in stages[:st] if z == "cffn")

                def cw(i, tile, tap):
                    if isinstance(i, int):
                        return par_("fcw", ((ci * 44 + 2 * i + tile) * 4) + tap, 1)
                    return par_("fcw", i * 8 + (ci * 44 + tile) * 4 + tap, 1)

                def taps(i, up):
                    b, dst = bank[5 if up else 4], cu if up else cg
                    k.wait("cid", st, i, 2, up)
                    for tap, name in ((1, "tap1"), (0, "tap2")):
                        lag = 2 - tap
                        if tap == 0:
                            k.wait("tap1", st, i, 2, up)
                        for m in range(2):
                            ins = eng.scalar_tensor_tensor(
                                out=dst[:, m, lag:T], in0=b[:, m * T:(m + 1) * T - lag],
                                scalar=cw(i, 22 * up + m, tap), in1=dst[:, m, lag:T], op0=ALU.mult, op1=ALU.add)
                        k.inc(name, ins)

                def gate(i, a, b, loop):
                    split(st, i, a, b, loop)
                    taps(i, 0)

                def up(i, a, b, loop):
                    split(st, i, a, b, loop)
                    taps(i, 1)
                    k.wait("silu", st, i, 1, 0)
                    k.wait("alo", st, i, 1, -1)
                    k.wait("tap2", st, i, 2, 1)
                    k.inc("mul", eng.tensor_tensor(act, sg, cu, ALU.mult))

                def lo(i):
                    k.wait("ahi", st, i, 1, 0)
                    k.inc("alo", eng.tensor_tensor(a_lo[:, :, :], act, a_hi[:, :, :], ALU.subtract))

                def down(i, a, b, loop):
                    split(st, i, a, b, loop)
                    lo(i)

                gate(0, 0, 0, None)
                up(0, 0, 1, None)
                lo(0)
                for i in k.loop(1, NFB - 1):
                    r = (1, NFB - 1)
                    gate(i, 3, -1, r)
                    up(i, 3, 0, r)
                    down(i, 3, 1, r)
                n = NFB - 1
                gate(n, 3, -1, None)
                up(n, 3, 0, None)
                down(n, 3, 1, None)
                split(st, 0, 0, 3 * n + 2)

            def mamba(st):
                two = dict(a=2)
                k.inc("sq0", eng.memset(sqa, 0.0))
                k.wait("dtp", st)
                step = [0]

                def dt_step(ins, wait=True):
                    k.inc("dta", ins)
                    step[0] += 1
                    if wait:
                        k.wait("dta", st, b=step[0] - 1)

                dt_step(eng.tensor_tensor(dv.rearrange("p (a h) -> p a h", a=2),
                                          bank[7][:, 0:64].rearrange("p (a h) -> p a h", a=2),
                                          par_("dtb").unsqueeze(1).to_broadcast([P, 2, 32]), ALU.add), False)
                k.wait("dtx", st, b=1)
                dt_step(eng.tensor_scalar(dw, de, 1.0, None, ALU.add))
                k.wait("dtx", st, b=2)
                dt_step(eng.tensor_scalar(dw, dw, 1.0, None, ALU.subtract))
                dt_step(eng.tensor_scalar(dm, dw, 0.0, None, ALU.is_equal))
                dt_step(eng.tensor_tensor(dw, dw, dm, ALU.add))
                dt_step(eng.reciprocal(dw, dw))
                dt_step(eng.tensor_tensor(dl, dl, dm, ALU.add))
                dt_step(eng.tensor_tensor(dl, dl, dw, ALU.mult))
                dt_step(eng.tensor_tensor(dl, dl, de, ALU.mult))
                dt_step(eng.scalar_tensor_tensor(out=dtt, in0=dv, scalar=0.0, in1=dl, op0=ALU.max, op1=ALU.add))
                k.wait("dtx", st, b=3)
                dt_step(eng.scalar_tensor_tensor(
                    out=dta.rearrange("p (a h) -> p a h", a=2), in0=dtt.rearrange("p (a h) -> p a h", a=2),
                    scalar=-1.0, in1=ea.unsqueeze(1).to_broadcast([P, 2, 32]), op0=ALU.mult, op1=ALU.mult), False)
                dt3 = dtt.rearrange("p (a h) -> p a h", a=2)

                def cum():
                    k.wait("acp", st)
                    k.inc("acv", eng.tensor_scalar(nac, bank[7][:, 64:128], -1.0, None, ALU.mult))
                    eng.tensor_copy(acT[:, 0:T], bank[6][0:32, 0:T])
                    k.inc("acv", eng.tensor_copy(acT[:, T:384], bank[6][0:32, P:T]))

                def taps(i, which, dst, b):
                    k.wait("cid", st, i, 2, which)
                    for n, tap in enumerate((2, 1, 0)):
                        lag = 3 - tap
                        if n:
                            k.wait("tap", st, i, 6, 3 * which + n - 1)
                        for m in range(2):
                            ins = eng.scalar_tensor_tensor(
                                out=dst[:, m, lag:T], in0=b[:, m * T:(m + 1) * T - lag],
                                scalar=par_("cw", i * 20 + (2 * which + m) * 5 + tap, 1),
                                in1=dst[:, m, lag:T], op0=ALU.mult, op1=ALU.add)
                        k.inc("tap", ins)

                def weigh(i, off, h):
                    k.wait("dec", st, i, 4, 4 * off + h)
                    if h == 0:
                        k.wait("cbs", st, i, 1, off)
                    k.inc("wv", eng.tensor_tensor(S[:, h, :], S[:, h, :], cbs, ALU.mult))

                def y_parts(i):
                    k.wait("yc", st, i, 1, -1)
                    k.inc("y1", eng.tensor_tensor(yb, bank[6][:, :].rearrange("p (a t) -> p a t", **two), dx, ALU.add))
                    k.wait("y1", st, i, 1, -1)
                    k.wait("sil", st, i, 3, -1)
                    k.inc("yz", eng.tensor_tensor(yb, yb, zc, ALU.mult))
                    k.wait("yz", st, i, 1, -1)
                    for m in range(2):
                        at = i * 2 + (m - 2)
                        ins = eng.tensor_scalar(yn[:, m, :], yb[:, m, :], par_("ngw", at, 1), None, ALU.mult)
                    k.inc("yn", ins)
                    k.wait("ysq", st, i, 1, -1)
                    k.wait("sq0", st)
                    k.wait("yac", st, i, 1, -2)
                    k.inc("yac", eng.tensor_tensor(sqa, sqa, sqt, ALU.add))

                def lo(i):
                    k.wait("ahi", st, i, 1, -1)
                    k.inc("alo", eng.tensor_tensor(a_lo[:, :, :], yn, a_hi[:, :, :], ALU.subtract))

                def body(i, loop, a, b):
                    more = not isinstance(i, int) or i > 0
                    split(st, i, a, b, loop)
                    taps(i, 0, xc, bank[4])
                    if more:
                        weigh(i, -1, 2)
                        weigh(i, -1, 3)
                    split(st, i, a, b + 1, loop)
                    taps(i, 1, bc, bank[5])
                    if not more:
                        cum()
                        k.wait("acv", st, b=1)
                    else:
                        k.wait("br", st, i, 4, -1)
                    gm = CONSTS["gmask"][0]
                    col = con[0:32, gm:gm + 1] if not more else con[0:32, bass.ds(i + gm, 1)]
                    k.inc("acg", eng.tensor_scalar(acg, acT, col, None, ALU.mult))
                    split(st, i, a, b + 2, loop)
                    if more:
                        y_parts(i)
                        split(st, i, a, b + 3, loop)
                        lo(i)
                    k.wait("sil", st, i, 3, 0)
                    for m in range(2):
                        ins = eng.tensor_scalar(dx[:, m, :], xc[:, m, :], par_("dskip", i * 2 + m, 1), None, ALU.mult)
                    k.inc("dx", ins)
                    k.wait("xt", st, i, 1, 0)
                    heads4 = dt3[:, :, 4 * i:4 * i + 4] if not more else dt3[:, :, bass.ds(i * 4, 4)]
                    k.inc("xdt", eng.tensor_tensor(
                        xdt.rearrange("p a (h c) -> p a h c", h=4),
                        bank[4][:, :].rearrange("p (a h c) -> p a h c", a=2, h=4),
                        heads4.unsqueeze(3).to_broadcast([P, 2, 4, HD]), ALU.mult))
                    k.wait("cb", st, i, 1, 0)
                    k.inc("cbs", eng.tensor_copy(cbs, bank[5][:, 0:384]))
                    weigh(i, 0, 0)
                    weigh(i, 0, 1)

                n = GROUPS["mamba"]
                body(0, None, 0, 0)
                for i in k.loop(1, n):
                    body(i, (1, n), 4, -1)
                weigh(n, -1, 2)
                weigh(n, -1, 3)
                y_parts(n)
                lo(n)
                split(st, 0, 0, 4 * n - 1)

            def heads(st, kind):
                n = GROUPS[kind]
                scale = 0.125 if kind == "moba" else 1.0

                def softmax(i, h):
                    k.wait("sc", st, i, 4, h)
                    b = bank[4 + h]
                    if kind == "moba":
                        sl = CONSTS["slope8"][0]
                        col = con[:, sl + 4 * i + h:sl + 4 * i + h + 1] if isinstance(i, int) else \
                            con[:, bass.ds(i * 4 + (sl + h), 1)]
                        k.inc("lg", eng.scalar_tensor_tensor(out=S[:, h, :], in0=con_("dist"), scalar=col,
                                                             in1=b[:, 0:384], op0=ALU.mult, op1=ALU.add))
                    elif kind == "dsa":
                        if h == 0:
                            k.wait("qlr", st, i, 2, 1)
                            base = plan.base["lg"][st] // 4
                            eng.wait_ge(s_bias, i * 16 + 16)
                        for c0, c1, tt, bb in ((0, 128, 0, 128), (128, 384, 1, 0)):
                            ins = eng.scalar_tensor_tensor(
                                out=S[:, h, c0:c1], in0=b[:, c0:c1], scalar=rq[:, 2 * h + tt:2 * h + tt + 1],
                                in1=bias[:, h, bb:bb + c1 - c0], op0=ALU.mult, op1=ALU.add)
                        k.inc("lg", ins)
                    else:
                        k.inc("lg", eng.tensor_copy(S[:, h, :], b[:, 0:384]))
                        return
                    k.wait("lg", st, i, 4, h)
                    eng.tensor_reduce(mxt[:, 2 * h:2 * h + 1], S[:, h, 0:128], AX.X, ALU.max)
                    k.inc("mx", eng.tensor_reduce(mxt[:, 2 * h + 1:2 * h + 2], S[:, h, 128:384], AX.X, ALU.max))
                    k.wait("mx", st, i, 4, h)
                    k.inc("nm", eng.tensor_scalar(nmx[:, 2 * h:2 * h + 2], mxt[:, 2 * h:2 * h + 2], -scale, None,
                                                  ALU.mult))

                def finish(i, h):
                    if kind == "sb":
                        k.wait("la", st, i, 4, h)
                        k.inc("lk", eng.scalar_tensor_tensor(out=LK[:, h, :], in0=S[:, h, :], scalar=0.0,
                                                             in1=LK[:, h, :], op0=ALU.max, op1=ALU.add))
                        k.wait("lk", st, i, 4, h)
                        for c in (0, 256):
                            ins = eng.tensor_tensor(LK[:, h, c:c + P], LK[:, h, c:c + P], con_("strict"), ALU.mult)
                        k.inc("prb", ins)
                        return
                    k.wait("ex", st, i, 4, h)
                    k.inc("rc", eng.reciprocal(rcp[:, 2 * h:2 * h + 2], sums[:, 2 * h:2 * h + 2]))
                    k.wait("rc", st, i, 4, h)
                    for c0, c1, tt in ((0, 128, 0), (128, 384, 1)):
                        ins = eng.tensor_scalar(S[:, h, c0:c1], S[:, h, c0:c1], rcp[:, 2 * h + tt:2 * h + tt + 1],
                                                None, ALU.mult)
                    k.inc("prb", ins)

                def arg(i, h):
                    if kind == "sb":
                        k.wait("ptp", st, i, 4, h - 4)
                        k.inc("arg", eng.tensor_tensor(S[:, h, :], S[:, h, :], bank[7 - h % 2][:, 0:384], ALU.subtract))

                def out_lo(i, p):
                    k.wait("ahi", st, i, 2, p - 2)
                    b = bank[5 if kind == "dsa" else 4]
                    k.inc("alo", eng.tensor_tensor(a_lo[:, p, :], b[:, p * T:(p + 1) * T], a_hi[:, p, :],
                                                   ALU.subtract))

                def body(i, loop, a, b, more):
                    split(st, i, a, b, loop)
                    split(st, i, a, b + 1, loop)
                    if more:
                        arg(i, 0)
                        arg(i, 1)
                    if kind == "dsa":
                        if more:
                            out_lo(i, 0)
                            out_lo(i, 1)
                            split(st, i, a, b + 2, loop)
                    else:
                        split(st, i, a, b + 2, loop)
                        if more:
                            out_lo(i, 0)
                            arg(i, 2)
                            arg(i, 3)
                            out_lo(i, 1)
                            split(st, i, a, b + 3, loop)
                    softmax(i, 0)
                    for h in range(4):
                        if h < 3:
                            softmax(i, h + 1)
                        finish(i, h)

                if kind == "dsa":
                    sparse_front(st)
                    body(0, None, 0, 3, False)
                    for i in k.loop(1, n):
                        body(i, (1, n), 3, 2, True)
                else:
                    body(0, None, 0, 0, False)
                    for i in k.loop(1, n):
                        body(i, (1, n), 4, -1, True)
                arg(n, 0)
                arg(n, 1)
                out_lo(n, 0)
                arg(n, 2)
                arg(n, 3)
                out_lo(n, 1)
                split(st, 0, 0, NBLK[kind] - 1)

            def sparse_front(st):
                k.wait("relp", st)
                k.inc("wiv", eng.tensor_scalar(wi, bank[7][:, 0:16].rearrange("p (a h) -> p a h", a=2), 8 ** -0.5,
                                               None, ALU.mult))
                k.inc("relv", eng.tensor_copy(relS, bank[7][0:16, P:512]))
                k.inc("gkq", eng.tensor_tensor(gkq, par_("qn"), par_("kn"), ALU.mult))
                k.inc("isc", eng.memset(isc, 0.0))
                split(st, b=0)
                split(st, b=1)
                k.wait("gkq", st)
                k.wait("klr", st, b=1)
                k.inc("kn", eng.scalar_tensor_tensor(out=kn, in0=latT, scalar=gkq, in1=rstd[:, :],
                                                     op0=ALU.mult, op1=ALU.mult))
                split(st, b=2)
                k.wait("wiv", st)
                for h in range(8):
                    k.wait("rel", st, b=h)
                    k.wait("isc", st, b=h)
                    for c0, c1, tt in ((0, 128, 0), (128, 384, 1)):
                        ins = eng.scalar_tensor_tensor(out=isc[:, c0:c1], in0=R[:, h % 2, c0:c1],
                                                       scalar=wi[:, tt, h:h + 1], in1=isc[:, c0:c1],
                                                       op0=ALU.mult, op1=ALU.add)
                    k.inc("isc", ins)
                k.wait("isc", st, b=8)
                k.inc("isc", eng.tensor_tensor(isc, isc, con_("causal"), ALU.add))
                k.wait("isc", st, b=9)
                n = 0
                for c0, c1 in ((0, 128), (128, 384)):
                    for r in range(8):
                        src = (wk if r else isc)[:, c0:c1]
                        k.inc("top", eng.max(v8, src))
                        k.wait("top", st, b=n)
                        k.inc("top", eng.match_replace(wk[:, c0:c1], v8, src, GONE))
                        k.wait("top", st, b=n + 1)
                        n += 2
                k.inc("msk", eng.tensor_scalar(isc, wk, -2e38, NEG, ALU.is_gt, ALU.mult))
                k.wait("msk", st)
                k.inc("msk", eng.tensor_tensor(maskb, isc, con_("causal"), ALU.add))

            programs = {"ffn": ffn, "cffn": cffn, "mamba": mamba, "moba": lambda st: heads(st, "moba"),
                        "sb": lambda st: heads(st, "sb"), "dsa": lambda st: heads(st, "dsa")}
            eng.wait_ge(sems["cact"], 1)
            for n in range(KT):
                eng.wait_ge(s_mo[n % 3], 16 * (n // 3 + 1))
                if n == 0:
                    ins = eng.tensor_scalar(macc[:, :], first_mod[0], cact[:, 0:1], None, ALU.mult)
                else:
                    eng.wait_ge(sems["mo"], n)
                    ins = eng.scalar_tensor_tensor(out=macc[:, :], in0=first_mod[n % 3], scalar=cact[:, n:n + 1],
                                                   in1=macc[:, :], op0=ALU.mult, op1=ALU.add)
                ins.then_inc(sems["mo"], 1)
            for b in range(-AHEAD, 0):
                split(0, b=b)
            modulation(0)
            for st, kind in enumerate(stages):
                norm(st)
                programs[kind](st)
                if st + 1 < NST:
                    modulation(st + 1)
                residual(st)

        @block.tensor
        def _(eng):
            k = Steps(eng, plan, sems)

            def begin(st, i, a, b, it):
                g, s, _ = k.block(st, i, a, b, it)
                eng.wait_ge(sems["wlo"], g + 1)
                hi = w_hi[s][:, :].rearrange("p (k n) -> p k n", k=KT)
                lo = w_lo[s][:, :].rearrange("p (k n) -> p k n", k=KT)
                return s, hi, lo

            def three(dst, ah, al, bh, bl, start, stop, skip=False):
                eng.matmul(dst, ah, bh, start=start, stop=False, skip_group_check=skip)
                eng.matmul(dst, ah, bl, start=False, stop=False, skip_group_check=skip)
                return eng.matmul(dst, al, bh, start=False, stop=stop, skip_group_check=skip)

            def gemm(dst, st, i=0, a=0, b=0, it=None, tokens=False, first=False):
                s, hi, lo = begin(st, i, a, b, it)
                for m in range(2):
                    for kk in range(KT):
                        if first and m == 0:
                            k.wait("hlo", st, b=kk)
                        part = slice(m * P, (m + 1) * P)
                        d = dst[:, m * T:(m + 1) * T]
                        if tokens:
                            mm = three(d, h_hi[:, kk, part], h_lo[:, kk, part], hi[:, kk, :], lo[:, kk, :],
                                       kk == 0, kk == KT - 1)
                        else:
                            mm = three(d, hi[:, kk, part], lo[:, kk, part], h_hi[:, kk, :], h_lo[:, kk, :],
                                       kk == 0, kk == KT - 1)
                mm.then_inc(sems["blk"], 1)

            def gemm_out(st, i=0, a=0, b=0, it=None, ready=None):
                s, _, _ = begin(st, i, a, b, it)
                hi = w_hi[s][:, :].rearrange("p (k n) -> p k n", k=2)
                lo = w_lo[s][:, :].rearrange("p (k n) -> p k n", k=2)
                for kk in range(2):
                    ready(kk)
                    for m in range(KT):
                        part = slice(m * P, (m + 1) * P)
                        mm = three(acc(m), hi[:, kk, part], lo[:, kk, part], a_hi[:, kk, :], a_lo[:, kk, :],
                                   False, False, True)
                mm.then_inc(sems["blk"], 1)

            def modulation(st):
                if st:
                    eng.wait_ge(sems["macc"], 31 * st)
                else:
                    eng.wait_ge(sems["mo"], KT)
                for c in range(24):
                    mm = eng.matmul(bank[7][:, c:c + 1], macc[:, c * P:(c + 1) * P], con_("ones")[:, 0:1],
                                    start=True, stop=True)
                k.inc("mods", mm)

            def norm(st):
                for rnd in range(2 if st == RESCALED else 1):
                    for m in range(KT):
                        k.wait("sq", st, b=8 * rnd + m)
                        mm = eng.matmul(bank[6][:, 0:T], con_("ones"), work3[:, m, :],
                                        start=m == 0, stop=m == KT - 1)
                    k.inc("ss", mm)
                if st:
                    k.wait("xup", st - 1, b=7)
                for n in range(4):
                    mm = eng.matmul(bank[n][:, :], ident_b, zero_b, start=True, stop=True)
                k.inc("zero", mm)

            def ffn(st):
                kind = stages[st]
                free4, per4, free5, per5 = ("silu", 1, "mul", 1) if kind == "ffn" else ("tap2", 2, "tap2", 2)

                def gate(i, a, b, loop, first=False):
                    if not first:
                        k.wait(free4, st, i, per4, -per4)
                    gemm(bank[4], st, i, a, b, loop, first=first)

                def up(i, a, b, loop, first=False):
                    if not first:
                        k.wait(free5, st, i, per5, -1)
                    gemm(bank[5], st, i, a, b, loop)

                def down(i, a, b, loop):
                    gemm_out(st, i, a, b, loop, lambda kk: k.wait("alo", st, i, 1, -1) if kk == 0 else None)

                gate(0, 0, 0, None, True)
                up(0, 0, 1, None, True)
                for i in k.loop(1, NFB - 1):
                    r = (1, NFB - 1)
                    gate(i, 3, -1, r)
                    up(i, 3, 0, r)
                    down(i, 3, 1, r)
                n = NFB - 1
                gate(n, 3, -1, None)
                up(n, 3, 0, None)
                down(n, 3, 1, None)
                last(st, lambda: k.wait("alo", st, b=n))

            def last(st, ready):
                if st + 1 < NST:
                    k.wait("modv", st, b=0)
                    modulation(st + 1)
                gemm_out(st, b=NBLK[stages[st]] - 1, ready=lambda kk: ready() if kk == 0 else None)

            def mamba(st):
                k.wait("hlo", st, b=KT - 1)
                for tt in range(2):
                    for kk in range(KT):
                        part = slice(tt * P, (tt + 1) * P)
                        ws = slice(40 * kk, 40 * kk + 32)
                        mm = three(bank[7][:, 32 * tt:32 * tt + 32], h_hi[:, kk, part], h_lo[:, kk, part],
                                   ws_hi[:, ws], ws_lo[:, ws], kk == 0, kk == KT - 1)
                k.inc("dtp", mm)
                tri, ones = con_("tri"), con_("ones")

                def cum():
                    k.wait("dta", st, b=10)
                    d0, d1 = dta[:, 0:32], dta[:, 32:64]
                    eng.matmul(bank[7][:, 64:96], tri, d0, start=True, stop=True)
                    eng.matmul(bank[7][:, 96:128], ones, d0, start=True, stop=False)
                    eng.matmul(bank[7][:, 96:128], tri, d1, start=False, stop=True)
                    eng.matmul(bank[6][0:32, 0:P], d0, tri, start=True, stop=True)
                    eng.matmul(bank[6][0:32, P:T], d0, ones, start=True, stop=False)
                    k.inc("acp", eng.matmul(bank[6][0:32, P:T], d1, tri, start=False, stop=True))

                def rows(i, off, h, free):
                    free()
                    b = bank[6 + h % 2]
                    sel = con_("selmod", 32)[:, h * P:(h + 1) * P]
                    eng.matmul(b[:, 0:384], sel, acg, start=True, stop=False, skip_group_check=True)
                    diag = b[:, :].rearrange("p (a b c) -> p a b c", a=2, b=2)[:, :, 0, :]
                    k.inc("br", eng.matmul(diag, ident_b, below_b.unsqueeze(1).to_broadcast([P, 2, P]),
                                           start=False, stop=True, skip_group_check=True))

                def parts(i):
                    k.wait("sil", st, i, 3, 0)
                    for m in range(2):
                        for tt in range(2):
                            mm = eng.transpose(bank[4][:, tt * T + m * P:tt * T + (m + 1) * P],
                                               xc[:, m, tt * P:(tt + 1) * P], con_("ident"))
                    k.inc("xt", mm)
                    k.wait("sil", st, i, 3, 1)
                    eng.matmul(bank[5][:, 0:T], bc[:, 0, 0:P], bc[:, 1, :], start=True, stop=True)
                    k.inc("cb", eng.matmul(bank[5][:, T:384], bc[:, 0, P:T], bc[:, 1, P:T], start=True, stop=True))
                    k.wait("acg", st, i, 1, 0)
                    rows(i, 0, 0, lambda: k.wait("y1", st, i, 1, -1))
                    rows(i, 0, 1, lambda: k.wait("sil", st, i, 3, 2))

                def more_rows(i):
                    rows(i, -1, 2, lambda: k.wait("dec", st, i, 4, -4))
                    rows(i, -1, 3, lambda: k.wait("dec", st, i, 4, -3))

                def y_out(i):
                    k.wait("dec", st, i, 4, -2)
                    k.wait("xdt", st, i, 1, -1)
                    for h in range(4):
                        k.wait("wv", st, i, 4, h - 4)
                        rows_, c0 = slice(HD * (h % 2), HD * (h % 2) + HD), (h // 2) * T
                        ch = slice(h * HD, (h + 1) * HD)
                        eng.matmul(bank[6][rows_, c0:c0 + T], xdt[:, 0, ch], S[:, h, 0:T], start=True, stop=False)
                        mm = eng.matmul(bank[6][rows_, c0 + P:c0 + T], xdt[:, 1, ch], S[:, h, T:384],
                                        start=False, stop=True)
                    k.inc("yc", mm)

                def body(i, loop, a, b):
                    more = not isinstance(i, int) or i > 0
                    k.wait("xdt", st, i, 1, -1)
                    gemm(bank[4], st, i, a, b, loop)
                    if more:
                        more_rows(i)
                    k.wait("cbs", st, i, 1, -1)
                    gemm(bank[5], st, i, a, b + 1, loop)
                    if more:
                        y_out(i)
                        k.wait("dec", st, i, 4, -1)
                    else:
                        cum()
                        k.wait("acv", st, b=1)
                    gemm(bank[7], st, i, a, b + 2, loop)
                    if more:
                        gemm_out(st, i, a, b + 3, loop, lambda kk: k.wait("alo", st, i, 1, -1) if kk == 0 else None)
                    parts(i)

                n = GROUPS["mamba"]
                body(0, None, 0, 0)
                for i in k.loop(1, n):
                    body(i, (1, n), 4, -1)
                more_rows(n)
                y_out(n)
                k.wait("yac", st, b=n - 1)
                eng.matmul(bank[6][:, 0:T], ones, sqa[:, 0, :], start=True, stop=False)
                k.inc("rs2p", eng.matmul(bank[6][:, 0:T], ones, sqa[:, 1, :], start=False, stop=True))
                k.wait("dec", st, b=4 * n - 1)
                last(st, lambda: k.wait("alo", st, b=n - 1))

            def heads(st, kind):
                n = GROUPS[kind]

                def scores(i):
                    free = {4: ("alo", 2, -1), 5: ("vev", 1, 0), 6: ("ptc", 4, -1), 7: ("ptc", 4, -2)}
                    if kind == "sb":
                        free[6], free[7] = ("arg", 4, -1), ("arg", 4, -2)
                    if kind == "dsa":
                        free[5] = ("alo", 2, -1)
                    k.wait("qev" if kind != "dsa" else "qev2", st, i, 1, 0)
                    if kind != "dsa":
                        k.wait("kev", st, i, 1, 0)
                    else:
                        k.wait(*free[7][:1], st, i, *free[7][1:])
                        for h in range(4):
                            if h % 2 == 0:
                                k.wait("qsq", st, i, 2, h // 2)
                            for tt in range(2):
                                q2 = qsq[h // 2][:, (h % 2) * T + tt * P:(h % 2) * T + (tt + 1) * P]
                                mm = eng.matmul(bank[7][:, 2 * h + tt:2 * h + tt + 1], q2, con_("ones")[:, 0:1],
                                                start=True, stop=True)
                        k.inc("qss", mm)
                    for h in range(4):
                        b = bank[4 + h]
                        k.wait(free[4 + h][0], st, i, *free[4 + h][1:])
                        r, m = slice(HD * (h % 2), HD * (h % 2) + HD), h // 2
                        if kind == "moba":
                            eng.matmul(b[:, 0:P], Q[r, m, 0:P], KB[r, m, 0:P], start=True, stop=True)
                            mm = eng.matmul(b[:, P:384], Q[r, m, P:T], KB[r, m, :], start=True, stop=True)
                        elif kind == "sb":
                            eng.matmul(b[:, 0:T], KB[r, m, 0:P], Q[r, m, :], start=True, stop=True)
                            mm = eng.matmul(b[:, T:384], KB[r, m, P:T], Q[r, m, P:T], start=True, stop=True)
                        else:
                            if h == 3:
                                k.wait("qlr", st, i, 2, 1)
                            eng.matmul(b[:, 0:P], Q[:, h, 0:P], kn[:, 0:P], start=True, stop=False,
                                       skip_group_check=True)
                            eng.matmul(b[:, P:384], Q[:, h, P:T], kn, start=False, stop=False, skip_group_check=True)
                            mm = eng.matmul(b[:, 0:384], ident_b, maskb, start=False, stop=True,
                                            skip_group_check=True)
                        k.inc("sc", mm)

                def turn(i, h):
                    k.wait("prb", st, i, 4, h - 4)
                    name = "arg" if kind == "sb" else "ptc"
                    if h >= 2:
                        k.wait(name, st, i, 4, h - 6)
                    else:
                        k.wait("lg", st, i, 4, 3 - h - 4)
                    b = bank[7 - h % 2]
                    if kind == "sb":
                        keep, triL = LK[:, h, :], con_("triL")
                        eng.matmul(b[:, 0:T], triL, keep[:, 0:T], start=True, stop=False, skip_group_check=True)
                        eng.matmul(b[:, P:T], con_("ones"), keep[:, T:384], start=False, stop=False,
                                   skip_group_check=True)
                        eng.matmul(b[:, T:384], triL, keep[:, T:384], start=False, stop=False, skip_group_check=True)
                        diag = b[:, :].rearrange("p (a b c) -> p a b c", a=2, b=2)[:, :, 0, :]
                        mm = eng.matmul(diag, ident_b, above_b.unsqueeze(1).to_broadcast([P, 2, P]),
                                        start=False, stop=True, skip_group_check=True)
                    else:
                        for c in range(3):
                            mm = eng.transpose(b[:, c * P:(c + 1) * P], S[:, h, c * P:(c + 1) * P], con_("ident"))
                    k.inc("ptp", mm)

                def values(i, p):
                    if kind != "dsa":
                        k.wait("vev", st, i, 1, -1)
                    if p and kind != "dsa":
                        k.wait("alo", st, i, 2, -2)
                    if p and kind == "dsa":
                        k.wait("ol", st, i, 2, -2)
                    for h in (2 * p, 2 * p + 1):
                        k.wait("ptc", st, i, 4, h - 4)
                        pr = PT[:, h % 2, :]
                        if kind == "dsa":
                            d, v = bank[4][:, (h % 2) * T:(h % 2 + 1) * T], [ltok[:, tt, :] for tt in range(2)]
                        else:
                            d = bank[4][HD * (h % 2):HD * (h % 2) + HD, p * T:(p + 1) * T]
                            v = [VB[:, tt, h * HD:(h + 1) * HD] for tt in range(2)]
                        eng.matmul(d, v[0], pr[:, 0:T], start=True, stop=False)
                        mm = eng.matmul(d[:, P:T], v[1], pr[:, T:384], start=False, stop=True)
                    k.inc("pv", mm)

                def lift(i, p):
                    k.wait("ol", st, i, 2, p - 2)
                    k.wait("wu", st, i, 1, -1)
                    if p:
                        k.wait("alo", st, i, 2, -2)
                    for j in range(2):
                        h = 2 * p + j
                        mm = eng.matmul(bank[5][HD * j:HD * j + HD, p * T:(p + 1) * T], wu[:, h * HD:(h + 1) * HD],
                                        OL[:, j, :], start=True, stop=True)
                    k.inc("olc", mm)

                def body(i, loop, a, b, more):
                    k.wait("lg", st, i, 4, -4)
                    gemm(bank[4], st, i, a, b, loop, first=not more and kind != "dsa")
                    if more:
                        turn(i, 0)
                        turn(i, 1)
                    k.wait("lg", st, i, 4, -3)
                    gemm(bank[5], st, i, a, b + 1, loop)
                    if more:
                        k.wait("qev", st, i, 1, 0)
                        values(i, 0)
                        turn(i, 2)
                        turn(i, 3)
                    if kind == "dsa":
                        if more:
                            k.wait("qev2", st, i, 1, 0)
                            lift(i, 0)
                            values(i, 1)
                            lift(i, 1)
                    else:
                        k.wait("kev", st, i, 1, 0)
                        gemm(bank[5], st, i, a, b + 2, loop, tokens=True)
                        if more:
                            values(i, 1)
                    if more:
                        gemm_out(st, i, a, b + (2 if kind == "dsa" else 3), loop,
                                 lambda kk: k.wait("alo", st, i, 2, kk - 2))
                    scores(i)

                if kind == "dsa":
                    sparse_front(st)
                    body(0, None, 0, 3, False)
                    for i in k.loop(1, n):
                        body(i, (1, n), 3, 2, True)
                else:
                    body(0, None, 0, 0, False)
                    for i in k.loop(1, n):
                        body(i, (1, n), 4, -1, True)
                turn(n, 0)
                turn(n, 1)
                values(n, 0)
                turn(n, 2)
                turn(n, 3)
                if kind == "dsa":
                    lift(n, 0)
                    values(n, 1)
                    lift(n, 1)
                else:
                    values(n, 1)
                k.wait("ptc", st, b=4 * n - 1)
                last(st, lambda: k.wait("alo", st, b=2 * n - 1))

            def sparse_front(st):
                k.wait("hlo", st, b=KT - 1)
                for tt in range(2):
                    for kk in range(KT):
                        part, ws = slice(tt * P, (tt + 1) * P), slice(40 * kk + 32, 40 * kk + 40)
                        mm = three(bank[7][:, 8 * tt:8 * tt + 8], h_hi[:, kk, part], h_lo[:, kk, part],
                                   ws_hi[:, ws], ws_lo[:, ws], kk == 0, kk == KT - 1)
                k.inc("wip", mm)
                o, _ = PARAMS["relb"]
                k.inc("relp", eng.matmul(bank[7][0:16, P:512], par[0:32, o:o + 16], con_("onehot", 32),
                                         start=True, stop=True))
                for n in range(3):
                    gemm(bank[4 + n], st, b=n)
                    if n == 1:
                        k.wait("relv", st)
                        k.wait("ksq", st)
                        k.inc("kss", eng.matmul(bank[7][:, 0:T], con_("ones"), qsq[0][:, 0:T], start=True, stop=True))
                k.wait("klr", st, b=1)
                for tt in range(2):
                    mm = eng.transpose(bank[7][:, tt * P:(tt + 1) * P], latT[:, tt * P:(tt + 1) * P], con_("ident"))
                k.inc("ltp", mm)
                k.wait("pre", st, b=2)
                for h in range(8):
                    if h >= 2:
                        k.wait("rel", st, b=h - 2)
                    b, r = bank[4 + h % 2], slice(HD * (h % 2), HD * (h % 2) + HD)
                    eng.matmul(b[:, 0:P], Q[r, h // 2, 0:P], ki2[r, 0:P], start=True, stop=True)
                    k.inc("ix", eng.matmul(b[:, P:384], Q[r, h // 2, P:T], ki2[r, :], start=True, stop=True))
                k.wait("ltc", st)
                k.wait("rel", st, b=7)
                k.wait("msk", st, b=1)
                k.wait("kn", st)

            programs = {"ffn": ffn, "cffn": ffn, "mamba": mamba, "moba": lambda st: heads(st, "moba"),
                        "sb": lambda st: heads(st, "sb"), "dsa": lambda st: heads(st, "dsa")}
            eng.wait_ge(sems["const"], 1)
            eng.wait_ge(sems["xst"], 2)
            modulation(0)
            for st, kind in enumerate(stages):
                norm(st)
                programs[kind](st)

        for name, n in plan.total.items():
            assert plan.tally.get(name, 0) == n, (name, plan.tally.get(name, 0), n)


def pack(inp):
    f = {k: np.asarray(v) for k, v in inp.items()}
    blocks = []

    def wide(w):
        n = w.shape[1] // 256
        return w.reshape(KT, P, n, 256).transpose(2, 1, 0, 3).reshape(n, P, 2048)

    def deep(w):
        n = w.shape[0] // 256
        return w.reshape(n, 2, P, D).transpose(0, 2, 1, 3).reshape(n, P, 2048)

    def pipelined(front, outs):
        n = len(outs)
        for i in range(n):
            blocks.extend(fr[i] for fr in front)
            if i:
                blocks.append(outs[i - 1])
        blocks.append(outs[n - 1])

    def ffn(i, j):
        pipelined([wide(f["ffn_w_gate"][i, j]), wide(f["ffn_w_up"][i, j])], deep(f["ffn_w_down"][i, j]))

    def cffn(i):
        w = f["ffn_w_up_2"][i]
        pipelined([wide(w[:, :DFF]), wide(w[:, DFF:])], deep(f["ffn_w_down_2"][i]))

    def attn(w, wo):
        pipelined([wide(w[:, :D]), wide(w[:, D:2 * D]), wide(w[:, 2 * D:])], deep(wo))

    def mamba():
        w = f["ssm_w_in"][0]
        z, xs, bm, cm = w[:, :2048], w[:, 2048:4096], w[:, 4096:5120], w[:, 5120:6144]
        bc = np.concatenate([bm.reshape(D, 8, P), cm.reshape(D, 8, P)], 2).reshape(D, 2048)
        pipelined([wide(xs), wide(bc), wide(z)], deep(f["ssm_w_out"][0]))

    def dsa():
        w = f["dsa_w_in_2"][0]
        q, lat, qi, ki = w[:, :2048], w[:, 2048:2176], w[:, 2176:2688], w[:, 2688:2752]
        blocks.extend(wide(np.concatenate([lat, ki, ki, qi], 1)))
        qb = wide(q)
        pipelined([qb[0::2], qb[1::2]], deep(f["dsa_w_out_2"][0]))

    ffn(0, 0)
    mamba()
    ffn(0, 1)
    ffn(1, 0)
    attn(f["attn_w_qkv"][0], f["attn_w_out"][0])
    ffn(1, 1)
    attn(f["sb_w_in_2"][0], f["sb_w_out_2"][0])
    cffn(0)
    dsa()
    cffn(1)
    weights = np.ascontiguousarray(np.stack(blocks))

    mods = np.concatenate([f["mod_w"].reshape(6, D, 3 * D),
                           f["ada_w_2"].reshape(2, D, 2, 3 * D).transpose(0, 2, 1, 3).reshape(4, D, 3 * D)])
    mods = mods.reshape(NJOB * KT, P, 3 * D)

    def col(v):
        return v.reshape(-1, P).T

    params = np.zeros((P, NPARAM), np.float32)

    def put(name, v):
        at, n = PARAMS[name]
        params[:v.shape[0], at:at + n] = v

    put("c", np.concatenate([col(f["c"][0])] * 6 + [col(f["c_2"][0])] * 4, 1))
    g2 = np.stack([f["norm_mix_2"], f["norm_ffn_2"]], 1).reshape(4, D)
    put("g", col(np.concatenate([f["norm_g"].reshape(6, D), g2])))
    put("gfin", col(f["final_norm_g"]))
    put("modb", col(np.concatenate([f["mod_b"].reshape(6, 3 * D), f["ada_b_2"].reshape(4, 3 * D)])))
    small = np.concatenate([f["ssm_w_in"][0][:, 6144:], f["dsa_w_in_2"][0][:, 2752:]], 1)
    put("wsmall", small.reshape(KT, P, 40).transpose(1, 0, 2).reshape(P, 320))
    put("dtb", np.broadcast_to(f["ssm_dt_bias"][0], (P, 32)))
    put("alog", np.broadcast_to(f["ssm_a_log"][0], (P, 32)))
    cw = np.concatenate([f["ssm_conv_w"][0][:, 0, :], f["ssm_conv_b"]]).reshape(5, 32, P)
    order = [t for g in range(8) for t in (2 * g, 2 * g + 1, 16 + g, 24 + g)]
    put("cw", cw[:, order, :].transpose(2, 1, 0).reshape(P, 160))
    put("dskip", col(np.repeat(f["ssm_d"][0], HD)))
    put("ngw", col(f["ssm_norm_w"][0]))
    fc = np.concatenate([f["ffn_conv_w_2"], f["ffn_conv_b_2"][:, None, :]], 1).reshape(2, 4, 44, P)
    put("fcw", fc.transpose(3, 0, 2, 1).reshape(P, 352))
    put("qn", f["dsa_q_norm_2"].T)
    put("kn", f["dsa_k_norm_2"].T)
    put("wuv", f["dsa_w_uv_2"][0].transpose(1, 0, 2).reshape(P, 1024))
    put("relb", f["rel_bias_2"])
    xin = f["x"][0].T.reshape(KT, P, T).transpose(1, 0, 2)
    return {"weights": weights, "mods": np.ascontiguousarray(mods), "params": params, "consts": constants(),
            "xin": np.ascontiguousarray(xin)}


def kernel(**inputs):
    import concourse.bacc as _bacc
    from concourse.bass_utils import run_bass_kernel_spmd as _run

    arrays = pack(inputs)
    nc = _bacc.Bacc("TRN2", target_bir_lowering=False, num_devices=1)
    args = [nc.dram_tensor(n, a.shape, F32, kind="ExternalInput").ap() for n, a in arrays.items()]
    out = nc.dram_tensor("out", (P, KT, T), F32, kind="ExternalOutput").ap()
    build(nc, *args, out)
    r = _run(nc, [arrays], core_ids=[0])
    got = r.results[0]["out"]
    return np.ascontiguousarray(got.transpose(2, 1, 0).reshape(1, T, D))
```

```python
from contextlib import ExitStack

import numpy as np
import concourse.bass as bass
from concourse import mybir

F32 = mybir.dt.float32
F32R = mybir.dt.float32r
BF16 = mybir.dt.bfloat16
ALU = mybir.AluOpType
ACT = mybir.ActivationFunctionType
AX = mybir.AxisListType

P = 128
T = 256
D = 1024
KT = D // P
DFF = 2816
HD = 64
NFB = DFF // 256
FOLD_AT = 8
GATE_AT = 1
AHEAD = 2
NSLOT = 4
EPS = 1e-6
NEG = -1e30
GONE = -3e38
EXP_LN = "natural_log_exp_and_others"
SILU = "silu_and_others"

STAGES = ["ffn", "mamba", "ffn", "ffn", "moba", "ffn", "sb", "cffn", "dsa", "cffn"]
NJOB = len(STAGES)
RESCALED = 6
GROUP_HEADS = 4
GROUPS = {"ffn": NFB, "cffn": NFB, "mamba": 8, "moba": 4, "sb": 4, "dsa": 4}
NBLK = {"ffn": 3 * NFB, "cffn": 3 * NFB, "mamba": 32, "moba": 16, "sb": 16, "dsa": 15}
RING = {"ffn": 3, "cffn": 3, "mamba": 4, "moba": 4, "sb": 4, "dsa": 3}

PARAM_COLS = [("c", NJOB * 8), ("g", NJOB * 8), ("gfin", 8), ("modb", NJOB * 24), ("wsmall", 8 * 40),
              ("dtb", 32), ("alog", 32), ("cw", 32 * 5), ("dskip", 16), ("ngw", 16), ("fcw", 2 * 44 * 4),
              ("qn", 1), ("kn", 1), ("wuv", 16 * 64), ("relb", 16)]
CONST_COLS = [("ones", P), ("tri", P), ("triL", P), ("ident", P),
              ("dist", 384), ("causal", 384), ("strict", P), ("slope8", 16), ("mod4", 4), ("gmask", 8), ("fold", P),
              ("onehot", 384)]


def offsets(cols):
    at, out = 0, {}
    for name, n in cols:
        out[name] = (at, n)
        at += n
    return out, at


PARAMS, NPARAM = offsets(PARAM_COLS)
CONSTS, NCONST = offsets(CONST_COLS)


def constants():
    p = np.arange(P)[:, None]
    c = np.arange(P)[None, :]
    big = np.arange(2 * P)[None, :]
    out = np.zeros((P, NCONST), np.float32)

    def put(name, v):
        at, n = CONSTS[name]
        out[:v.shape[0], at:at + n] = v

    put("ones", np.ones((P, P)))
    put("tri", p <= c)
    put("triL", p >= c)
    put("ident", p == c)
    causal = np.concatenate([c <= p, big <= p + P], 1)
    dist = np.concatenate([p - c, p + P - big], 1)
    put("dist", np.where(causal, -dist, NEG))
    put("causal", np.where(causal, 0, NEG))
    put("strict", p < c)
    put("fold", p % 32 == c % 32)
    put("slope8", np.broadcast_to(8.0 * 2.0 ** (-8.0 * (np.arange(16) + 1.0) / 16), (P, 16)))
    k = np.arange(64)[:, None] % 32
    put("mod4", k % 4 == np.arange(4)[None, :])
    put("gmask", k // 4 == np.arange(8)[None, :])
    n = np.maximum(255 - np.arange(384), 0)
    nf = np.maximum(n, 1).astype(np.float32)
    large = 16 + (np.log(nf / np.float32(16)) / np.float32(np.log(8.0)) * np.float32(16)).astype(np.int32)
    bucket = np.where(n < 16, n, np.minimum(large, 31))
    put("onehot", np.arange(32)[:, None] == bucket[None, :])
    return out


class Plan:

    def __init__(self, stages):
        self.stages = stages
        self.first = []
        self.slot, self.use = [], []
        used = [0] * NSLOT
        for kind in stages:
            self.first.append(len(self.slot))
            for n in range(NBLK[kind]):
                s = n % RING[kind]
                self.slot.append(s)
                self.use.append(used[s])
                used[s] += 1
        self.nblk = len(self.slot)
        self.base, self.tally = {}, {}
        total = {}
        for st, kind in enumerate(stages):
            for name, n in self.steps(st, kind).items():
                self.base.setdefault(name, {})[st] = total.get(name, 0)
                total[name] = total.get(name, 0) + n
            for name in total:
                self.base[name].setdefault(st, total[name])
        for name in total:
            for st in range(len(stages)):
                self.base[name].setdefault(st, 0)
            self.base[name][len(stages)] = total[name]
        self.total = total

    def steps(self, st, kind):
        g = GROUPS[kind]
        out = {"fold": 4, "mods": 1, "modv": 1, "pair": 3, "xup": 8, "sq": 8, "ss": 1, "ln": 1, "rstd": 1,
               "t": 8, "hhi": 8, "hlo": 8, "zero": 1, "ahi": 0, "alo": 0}
        if st == RESCALED:
            out |= {"sq": 16, "ln": 2, "rstd": 2, "ms2": 4, "xfin": 8}
        if kind in ("ffn", "cffn"):
            out |= {"silu": g, "mul": g, "ahi": g, "alo": g}
        if kind == "cffn":
            out |= {"cid": 2 * g, "tap1": 2 * g, "tap2": 2 * g}
        if kind == "mamba":
            out |= {"dtp": 1, "dta": 12, "dtx": 4, "acp": 1, "acv": 3, "sq0": 1, "cid": 2 * g, "tap": 6 * g,
                    "sil": 3 * g, "acg": g, "xt": g, "cb": g, "br": 4 * g, "xdt": g, "cbs": g, "dx": g,
                    "dec": 4 * g, "wv": 4 * g, "yc": g, "y1": g, "zw": g, "yz": g, "ysq": g, "yn": g, "yac": g,
                    "ahi": g, "alo": g, "rs2p": 1, "rs2": 2, "xr": 8}
        if kind in ("moba", "sb", "dsa"):
            out |= {"sc": 4 * g, "qev": g, "lg": 4 * g, "ptp": 4 * g, "ptc": 4 * g, "pv": 2 * g,
                    "ahi": 2 * g, "alo": 2 * g}
        if kind in ("moba", "sb"):
            out |= {"kev": g, "vev": g}
        if kind in ("moba", "dsa"):
            out |= {"mx": 4 * g, "nm": 4 * g, "ex": 4 * g, "rc": 4 * g, "prs": 4 * g}
        if kind == "sb":
            out |= {"ab": 4 * g, "ea": 4 * g, "la": 4 * g, "lk": 4 * g, "prb": 4 * g, "arg": 4 * g}
        if kind == "dsa":
            out |= {"qev2": g, "pre": 3, "wip": 1, "relp": 1, "wiv": 1, "relv": 1, "ix": 8, "rel": 8,
                    "isc": 10, "top": 32, "msk": 2, "ksq": 1, "kss": 1, "klr": 2, "gkq": 1, "kn": 1,
                    "ltp": 1, "ltc": 1, "qsq": 2 * g, "qss": g, "qlr": 2 * g, "ol": 2 * g, "olc": 2 * g, "wu": g}
        return out


class Steps:

    def __init__(self, eng, plan, sems):
        self.eng, self.plan, self.sems = eng, plan, sems
        self.trips = 1

    def loop(self, a, b):
        self.trips = b - a
        with self.eng.Fori(a, b) as i:
            yield i
        self.trips = 1

    def inc(self, name, ins):
        ins.then_inc(self.sems[name], 1)
        self.plan.tally[name] = self.plan.tally.get(name, 0) + self.trips
        return ins

    def wait(self, name, st, i=0, a=0, b=0):
        v = self.plan.base[name][st] + b + 1
        v = i * a + v if a else v
        if isinstance(v, int) and v <= 0:
            return
        self.eng.wait_ge(self.sems[name], v)

    def block(self, st, i=0, a=0, b=0, it=None):
        plan, at = self.plan, self.plan.first[st] + b
        if it is None:
            g = at + i * a
            if g >= plan.nblk:
                return None
            return g, plan.slot[g], plan.use[g]
        g0 = at + it[0] * a
        for n in range(*it):
            g = at + n * a
            assert plan.slot[g] == plan.slot[g0] and plan.use[g] == plan.use[g0] + n - it[0]
        return i * a + at, plan.slot[g0], i + (plan.use[g0] - it[0])


def build(nc, weights, mods, params, consts, xin, out, stages=None):
    stages = stages or STAGES
    plan = Plan(stages)
    NST = len(stages)
    with ExitStack() as ctx:
        def sb(name, shape, dt=F32):
            return ctx.enter_context(nc.sbuf_tensor(name, shape, dt))

        raw = [sb(f"raw{s}", [P, 2048]) for s in range(NSLOT)]
        w_hi = [sb(f"w_hi{s}", [P, 2048], F32R) for s in range(NSLOT)]
        w_lo = [sb(f"w_lo{s}", [P, 2048], F32R) for s in range(NSLOT)]
        x = sb("x", [P, KT, T])
        h_hi = sb("h_hi", [P, KT, T], F32R)
        h_lo = sb("h_lo", [P, KT, T], F32R)
        work = sb("work", [P, KT * T])
        work3 = work[:, :].rearrange("p (k t) -> p k t", k=KT)
        modws = sb("modws", [P, 3072])
        modw = [modws[:, 1536 * s:1536 * (s + 1)] for s in range(2)]
        macc = sb("macc", [P, 3072])
        folded = sb("folded", [P, 96])
        modv = sb("modv", [P, NJOB, 24])
        gs = sb("gs", [P, NJOB, 8])
        par = sb("par", [P, NPARAM])
        con = sb("con", [P, NCONST])
        conb = sb("conb", [P, 4 * P + 384], BF16)
        ws_hi = sb("ws_hi", [P, 8 * 40], F32R)
        ws_lo = sb("ws_lo", [P, 8 * 40], F32R)
        small = sb("small", [P, 4])
        cact = sb("cact", [P, NJOB * 8])
        cj = sb("cj", [P, 8])[:, :]
        rstd = sb("rstd", [P, T])
        sel = sb("sel", [64, 512], F32R)
        acg = sb("acg", [64, 384], F32R)[:, :]
        a_hi = sb("a_hi", [P, 2, T], F32R)
        a_lo = sb("a_lo", [P, 2, T], F32R)
        z_hi, z_lo = h_hi[:, 0:2, :], h_lo[:, 0:2, :]
        mix = sb("mix", [P, 6144])
        first_mod = [mix[:, 2048 * n:2048 * n + 2048] for n in range(3)] + [modws[:, 0:2048]]
        gatew = mix[:, 2048:6144].rearrange("p (a n) -> p a n", a=4)
        gacc, gtr = work[:, 0:1024], work[:, 1024:2048]
        gfold = sb("gfold", [P, 32])[:, :]
        bank = [ctx.enter_context(nc.psum_tensor(f"bank{n}", [P, 512], F32)) for n in range(8)]
        scratch = nc.dram_tensor("scratch", (16, 384), F32, kind="Internal").ap()
        biases = nc.dram_tensor("biases", (P, 16, T), F32, kind="Internal").ap()

        def sem(name):
            return ctx.enter_context(nc.semaphore("s_" + name))

        sems = {n: sem(n) for n in list(plan.total) + ["blk", "whi", "wlo", "macc", "const", "cact", "xst", "mo", "go", "gmods"]}
        s_raw = [sem(f"raw{s}") for s in range(NSLOT)]
        s_mo = [sem(f"mo{s}") for s in range(4)]
        s_gate = sem("gatew")
        s_modw = [sem(f"modw{s}") for s in range(2)]
        s_in, s_par, s_con, s_out, s_rel, s_bias = (sem(n) for n in ("in", "par", "con", "out", "relst", "bias"))

        def view(off, *dims):
            n = int(np.prod(dims))
            v = mix[:, off:off + n]
            if len(dims) == 2:
                v = v.rearrange("p (a b) -> p a b", a=dims[0])
            if len(dims) == 3:
                v = v.rearrange("p (a b c) -> p a b c", a=dims[0], b=dims[1])
            return v

        def par_(name, at=0, n=None):
            o, w = PARAMS[name]
            if isinstance(at, int):
                return par[:, o + at:o + at + (w if n is None else n)]
            return par[:, bass.ds(at + o, n)]

        def con_(name, rows=P):
            o, w = CONSTS[name]
            return con[0:rows, o:o + w]

        ident_b, below_b, above_b = conb[:, 0:P], conb[:, P:2 * P], conb[:, 2 * P:3 * P]
        zero_b = conb[:, 3 * P:4 * P]
        eps_c, eps128_c, one_c = small[:, 0:1], small[:, 1:2], small[:, 2:3]

        def acc(m):
            return bank[m // 2][:, (m % 2) * T:(m % 2 + 1) * T]

        sq2 = view(0, KT, T)
        rstd2 = mix[:, 2048:2304]
        sg = view(0, 2, T)
        act = view(512, 2, T)
        cg = view(1024, 2, T)
        cu = view(1536, 2, T)
        xc, bc, zc, dx = (view(512 * n, 2, T) for n in range(4))
        xdt = view(2048, 2, T)
        cbs = mix[:, 2560:2944]
        acT = mix[0:64, 4864:5248]
        yb = view(3328, 2, T)
        sqa = view(3840, 2, T)
        sqt = view(4352, 2, T)
        dtt, nac, dv, de, dw, dl, dm = (mix[:, 5248 + 64 * n:5312 + 64 * n] for n in range(7))
        dta = mix[:, 5696:5824].rearrange("p (a d h) -> p a d h", a=2, d=2)
        ea = mix[:, 5824:5856]
        r2 = mix[:, 5856:6112]
        yn = work[:, 1536:2048].rearrange("p (a t) -> p a t", a=2)
        Q = view(0, 4, T)
        KB = view(1024, 2, T)
        VB = view(1536, 2, T)
        PT = view(2048, 2, 384)
        mxt, nmx, sums, rcp = (mix[:, 2816 + 8 * n:2824 + 8 * n] for n in range(4))
        S = work[:, 0:1536].rearrange("p (h c) -> p h c", h=4)
        LK = view(3072, 4, 384)
        kn, ltok = mix[:, 1024:1280], view(1280, 2, P)
        wu = mix[:, 1536:1792]
        rq = mix[:, 1792:1800]
        wi = view(1800, 2, 8)
        gkq = mix[:, 1816:1817]
        v8 = [mix[:, 1824:1832], mix[:, 1832:1840]]
        OL = view(3072, 2, T)
        bias = view(3584, 4, T)
        maskb = conb[:, 4 * P:4 * P + 384]
        latT, ki2 = mix[:, 2048:2304], mix[:, 3072:3328]
        R = view(4608, 2, 384)
        isc, wk = mix[:, 5376:5760], mix[:, 5760:6144]
        relS = mix[0:16, 3584:3968]
        qsq = [work[:, 1536:2048], mix[:, 4608:5120]]

        block = ctx.enter_context(nc.Block())

        @block.sync
        def _(eng):
            k = Steps(eng, plan, sems)
            for n in range(KT):
                if n >= 4:
                    eng.wait_ge(sems["mo"], n - 3)
                eng.dma_start(first_mod[n % 4], mods[n][:, 0:2048]).then_inc(s_mo[n % 4], 16)
                if n == KT - 2:
                    eng.dma_start(x[:, :, :], xin).then_inc(s_in, 16)
            eng.dma_start(con[:, :], consts).then_inc(s_con, 16)

            def load(st, i, a, b, it=None, wait=True):
                g, s, _ = k.block(st, i, a, b, it)
                if wait:
                    eng.wait_ge(sems["wlo"], g - 2)
                src = weights[g] if it is None else weights[bass.ds(g, 1)].rearrange("a p n -> (a p) n")
                eng.dma_start(raw[s][:, :], src).then_inc(s_raw[s], 16)

            for st, kind in enumerate(stages):
                ring, n = RING[kind], NBLK[kind]
                a = 0
                if st == 0:
                    for b in range(ring):
                        load(st, 0, 0, b, wait=b >= 3)
                    a = 1
                for i in k.loop(a, n // ring):
                    for b in range(ring):
                        load(st, i, ring, b, (a, n // ring))
            for m in range(KT):
                eng.wait_ge(sems["xup"], plan.base["xup"][NST - 1] + m + 1)
                eng.dma_start(out[:, m, :], x[:, m, :]).then_inc(s_out, 16)
            eng.wait_ge(s_out, 16 * KT)

        @block.gpsimd
        def _(eng):
            k = Steps(eng, plan, sems)

            def load(q, half):
                src = mods[q] if isinstance(q, int) else mods[bass.ds(q, 1)].rearrange("a p n -> (a p) n")
                eng.dma_start(modw[half], src[:, half * 1536:(half + 1) * 1536]).then_inc(s_modw[half], 16)

            per = 1 + 2 + 4 * 7

            def job(j):
                j1, at = j - 1, 1
                eng.wait_ge(sems["fold"], j * 4)
                load(j * 8, 0)
                load(j * 8, 1)

                def step(ins):
                    nonlocal at
                    ins.then_inc(sems["macc"], 1)
                    eng.wait_ge(sems["macc"], j1 * per + at)
                    at += 1

                src = cact[:, 8 * j:8 * j + 8] if isinstance(j, int) else cact[:, bass.ds(j * 8, 8)]
                step(eng.tensor_copy(cj, src))
                for n in range(8):
                    for half in range(2):
                        eng.wait_ge(s_modw[half], j1 * 128 + (n + 1) * 16)
                        w, m = modw[half], macc[:, half * 1536:(half + 1) * 1536]
                        c = cj[:, n:n + 1].to_broadcast([P, 1536])
                        if n == 0:
                            step(eng.tensor_tensor(m, w, c, ALU.mult))
                        else:
                            step(eng.tensor_tensor(w, w, c, ALU.mult))
                            step(eng.tensor_tensor(m, m, w, ALU.add))
                        if n < 7:
                            load(j * 8 + (n + 1), half)

            if NST > 1:
                eng.wait_ge(sems["cact"], 1)
                for j in k.loop(1, NST):
                    job(j)

        @block.scalar
        def _(eng):
            k = Steps(eng, plan, sems)
            eng.dma_start(par[:, :], params).then_inc(s_par, 16)
            eng.wait_ge(s_par, 16)
            k.inc("cact", eng.activation(cact[:, :], par_("c"), ACT.Silu))

            def start():
                eng.wait_ge(s_con, 16)
                eng.activation(ident_b, con_("ident"), ACT.Copy)
                eng.activation(above_b, con_("triL"), ACT.Copy, scale=-NEG)
                m4 = con_("mod4", 64)
                eng.activation(sel[:, :].rearrange("p (h c) -> p h c", h=4), m4.unsqueeze(2).to_broadcast([64, 4, P]),
                               ACT.Copy)
                eng.activation(ws_hi[:, :], par_("wsmall"), ACT.Copy).then_inc(sems["const"], 1)
                for b in range(-AHEAD, 0):
                    split(0, b=b)
                gate_weights(0)

            def gate_weights(rnd):
                if rnd:
                    eng.wait_ge(sems["go"], 4)
                else:
                    eng.wait_ge(sems["mo"], KT)
                for n in range(4):
                    eng.dma_start(gatew[:, n, :], mods[4 * rnd + n][:, 2048:3072]).then_inc(s_gate, 16)

            def split(st, i=0, a=0, b=0, it=None):
                blk = k.block(st, i, a, b + AHEAD, it)
                if blk is None:
                    return
                g, s, use = blk
                eng.wait_ge(s_raw[s], use * 16 + 16)
                if it is not None or g >= 3:
                    eng.wait_ge(sems["blk"], g - 2)
                eng.activation(w_hi[s][:, :], raw[s][:, :], ACT.Copy).then_inc(sems["whi"], 1)

            def rs(out_, in_, scale, eps, name, st, i=0, a=0, b=0):
                k.inc(name[0], eng.activation(out_, in_, ACT.Ln, bias=eps, scale=scale))
                k.wait(name[0], st, i, a, b)
                return k.inc(name[1], eng.activation(out_, out_, ACT.Exp, scale=-0.5))

            def norm(st):
                eng.preload_act_table_set(EXP_LN)
                final = st == RESCALED
                for m in range(KT):
                    if st:
                        k.wait("xup", st - 1, b=m)
                    elif m == 0:
                        eng.wait_ge(s_in, 16)
                    k.inc("sq", eng.activation(work3[:, m, :], x[:, m, :], ACT.Square))
                    if final:
                        k.inc("sq", eng.activation(sq2[:, m, :], x[:, m, :], ACT.Square, scale=par_("gfin", m, 1)))
                if st == 0:
                    start()
                k.wait("ss", st)
                rs(rstd[:, :], bank[6][:, 0:T], 1.0 / D, eps_c, ("ln", "rstd"), st)
                if final:
                    k.wait("ms2", st, b=1)
                    rs(rstd2, rstd2, 1.0 / D, eps_c, ("ln", "rstd"), st, b=1)
                for m in range(KT):
                    k.wait("t", st, b=m)
                    k.inc("hhi", eng.activation(h_hi[:, m, :], work3[:, m, :], ACT.Identity,
                                                bias=modv[:, st, m:m + 1]))

            def ffn(st):
                def gate(i, a, b, loop):
                    split(st, i, a, b, loop)
                    eng.wait_ge(sems["blk"], k.block(st, i, a, b, loop)[0] + 1)
                    k.wait("mul", st, i, 1, -1)
                    k.inc("silu", eng.activation(sg, bank[4][:, :].rearrange("p (a t) -> p a t", a=2), ACT.Silu))

                def up(i, a, b, loop):
                    split(st, i, a, b, loop)

                def down(i, a, b, loop):
                    split(st, i, a, b, loop)
                    hi(i, a, b, loop)

                def hi(i, a, b, loop):
                    final = isinstance(i, int) and i == NFB - 1
                    if (a or b) and not final:
                        eng.wait_ge(sems["blk"], k.block(st, i, a, b, loop)[0] + 1)
                    k.wait("mul", st, i, 1, 0)
                    k.inc("ahi", eng.activation(z_hi if final else a_hi[:, :, :], act, ACT.Copy))

                gate(0, 0, 0, None)
                up(0, 0, 1, None)
                hi(0, 0, 0, None)
                begin = 1
                if st == 0:
                    for n in range(1, GATE_AT + 1):
                        gate(n, 3, -1, None)
                        up(n, 3, 0, None)
                        down(n, 3, 1, None)
                    gate_weights(1)
                    begin = GATE_AT + 1
                for i in k.loop(begin, NFB - 1):
                    r = (begin, NFB - 1)
                    gate(i, 3, -1, r)
                    up(i, 3, 0, r)
                    down(i, 3, 1, r)
                n = NFB - 1
                gate(n, 3, -1, None)
                up(n, 3, 0, None)
                down(n, 3, 1, None)
                split(st, 0, 0, 3 * n + 2)

            def cffn(st):
                ci = sum(1 for z in stages[:st] if z == "cffn")

                def cw(i, tile, tap):
                    if isinstance(i, int):
                        return par_("fcw", ((ci * 44 + 2 * i + tile) * 4) + tap, 1)
                    return par_("fcw", i * 8 + (ci * 44 + tile) * 4 + tap, 1)

                def taps(i, up):
                    b, dst = bank[5 if up else 4], cu if up else cg
                    k.wait("mul", st, i, 1, -1)
                    for m in range(2):
                        t = 22 * up + m
                        ins = eng.activation(dst[:, m, :], b[:, m * T:(m + 1) * T], ACT.Identity,
                                             scale=cw(i, t, 2), bias=cw(i, t, 3))
                    k.inc("cid", ins)

                def gate(i, a, b, loop):
                    split(st, i, a, b, loop)
                    eng.wait_ge(sems["blk"], k.block(st, i, a, b, loop)[0] + 1)
                    taps(i, 0)

                def up(i, a, b, loop):
                    split(st, i, a, b, loop)
                    k.wait("tap2", st, i, 2, 0)
                    k.inc("silu", eng.activation(sg, cg, ACT.Silu))
                    eng.wait_ge(sems["blk"], k.block(st, i, a, b, loop)[0] + 1)
                    taps(i, 1)

                def hi(i, a, b, loop):
                    final = isinstance(i, int) and i == NFB - 1
                    if (a or b) and not final:
                        eng.wait_ge(sems["blk"], k.block(st, i, a, b, loop)[0] + 1)
                    k.wait("mul", st, i, 1, 0)
                    k.inc("ahi", eng.activation(z_hi if final else a_hi[:, :, :], act, ACT.Copy))

                def down(i, a, b, loop):
                    split(st, i, a, b, loop)
                    hi(i, a, b, loop)

                gate(0, 0, 0, None)
                up(0, 0, 1, None)
                hi(0, 0, 0, None)
                for i in k.loop(1, NFB - 1):
                    r = (1, NFB - 1)
                    gate(i, 3, -1, r)
                    up(i, 3, 0, r)
                    down(i, 3, 1, r)
                n = NFB - 1
                gate(n, 3, -1, None)
                up(n, 3, 0, None)
                down(n, 3, 1, None)
                split(st, 0, 0, 3 * n + 2)

            def done(st, i, a, b, loop):
                eng.wait_ge(sems["blk"], k.block(st, i, a, b, loop)[0] + 1)

            def mamba(st):
                def timestep():
                    k.wait("dta", st, b=0)
                    k.inc("dtx", eng.activation(de, dv, ACT.Abs))
                    k.wait("dtx", st, b=0)
                    k.inc("dtx", eng.activation(de, de, ACT.Exp, scale=-1.0))
                    k.wait("dta", st, b=1)
                    k.inc("dtx", eng.activation(dl, dw, ACT.Ln))
                    k.inc("dtx", eng.activation(ea, par_("alog"), ACT.Exp))

                def conv(i, dst, b, first, free):
                    free()
                    for m in range(2):
                        t = first + m
                        sc, bi = (par_("cw", i * 20 + 5 * t + tap, 1) for tap in (3, 4))
                        ins = eng.activation(dst[:, m, :], b[:, m * T:(m + 1) * T], ACT.Identity, scale=sc, bias=bi)
                    k.inc("cid", ins)

                def silu(i, n, dst, src):
                    k.inc("sil", eng.activation(dst, src, ACT.Silu))

                def decay(i, off, h):
                    k.wait("br", st, i, 4, 4 * off + h)
                    if h == 0:
                        k.wait("yc", st, i, 1, off - 1)
                    b = bank[6 + h % 2]
                    for c0, c1, tt in ((0, 256, 0), (256, 384, 1)):
                        at = i * 4 + (4 * off + h)
                        nb = nac[:, 32 * tt + at:32 * tt + at + 1] if isinstance(at, int) else \
                            nac[:, bass.ds(at + 32 * tt, 1)]
                        ins = eng.activation(S[:, h, c0:c1], b[:, c0:c1], ACT.Exp, bias=nb)
                    k.inc("dec", ins)

                def body(i, loop, a, b):
                    more = not isinstance(i, int) or i > 0
                    split(st, i, a, b, loop)
                    done(st, i, a, b, loop)
                    conv(i, xc, bank[4], 0, lambda: (k.wait("xt", st, i, 1, -1), k.wait("dx", st, i, 1, -1)))
                    if more:
                        decay(i, -1, 2)
                        decay(i, -1, 3)
                    else:
                        timestep()
                    split(st, i, a, b + 1, loop)
                    k.wait("tap", st, i, 6, 2)
                    silu(i, 0, xc, xc)
                    done(st, i, a, b + 1, loop)
                    conv(i, bc, bank[5], 2, lambda: k.wait("cb", st, i, 1, -1))
                    split(st, i, a, b + 2, loop)
                    k.wait("tap", st, i, 6, 5)
                    silu(i, 1, bc, bc)
                    if more:
                        y_parts(i)
                    done(st, i, a, b + 2, loop)
                    k.wait("yz", st, i, 1, -1)
                    silu(i, 2, zc, bank[7][:, :].rearrange("p (a t) -> p a t", a=2))
                    if more:
                        split(st, i, a, b + 3, loop)
                    decay(i, 0, 0)
                    decay(i, 0, 1)

                def y_parts(i):
                    k.wait("yn", st, i, 1, -1)
                    k.inc("ahi", eng.activation(a_hi[:, :, :], yn, ACT.Copy))
                    k.wait("yz", st, i, 1, -1)
                    k.wait("yac", st, i, 1, -2)
                    k.inc("ysq", eng.activation(sqt, yb, ACT.Square))

                n = GROUPS["mamba"]
                body(0, None, 0, 0)
                for i in k.loop(1, n):
                    body(i, (1, n), 4, -1)
                decay(n, -1, 2)
                decay(n, -1, 3)
                y_parts(n)
                eng.preload_act_table_set(EXP_LN)
                split(st, 0, 0, 4 * n - 1)
                k.wait("rs2p", st)
                rs(r2, bank[6][:, 0:T], 1.0 / 2048, eps_c, ("rs2", "rs2"), st)

            def heads(st, kind):
                n = GROUPS[kind]
                scale = 0.125 if kind == "moba" else 1.0

                def softmax(i, h):
                    if kind == "sb":
                        if h == 0:
                            k.wait("ptp", st, i, 4, -1)
                        k.wait("lg", st, i, 4, h)
                        k.inc("ab", eng.activation(LK[:, h, :], S[:, h, :], ACT.Abs))
                        k.wait("ab", st, i, 4, h)
                        k.inc("ea", eng.activation(LK[:, h, :], LK[:, h, :], ACT.Exp, scale=-1.0))
                        k.wait("ea", st, i, 4, h)
                        k.inc("la", eng.activation(LK[:, h, :], LK[:, h, :], ACT.Ln, bias=one_c))
                        return
                    k.wait("nm", st, i, 4, h)
                    for c0, c1, tt in ((0, 128, 0), (128, 384, 1)):
                        ins = eng.activation(S[:, h, c0:c1], S[:, h, c0:c1], ACT.Exp, scale=scale,
                                             bias=nmx[:, 2 * h + tt:2 * h + tt + 1],
                                             accum_out=sums[:, 2 * h + tt:2 * h + tt + 1])
                    k.inc("ex", ins)

                def normalise(i, h):
                    if kind == "sb":
                        return
                    k.wait("rc", st, i, 4, h)
                    for c0, c1, tt in ((0, 128, 0), (128, 384, 1)):
                        ins = eng.activation(S[:, h, c0:c1], S[:, h, c0:c1], ACT.Copy,
                                             scale=rcp[:, 2 * h + tt:2 * h + tt + 1])
                    k.inc("prs", ins)

                def pt(i, h):
                    if h % 2 == 0:
                        k.wait("pv", st, i, 2, -2 + h // 2 - 1)
                    if kind == "sb":
                        k.wait("arg", st, i, 4, h - 4)
                        k.inc("ptc", eng.activation(PT[:, h % 2, :], S[:, h, :], ACT.Exp))
                    else:
                        k.wait("ptp", st, i, 4, h - 4)
                        k.inc("ptc", eng.activation(PT[:, h % 2, :], bank[7 - h % 2][:, 0:384], ACT.Copy))

                def out_hi(i, p, loop):
                    if kind == "dsa":
                        k.wait("olc", st, i, 2, p - 2)
                    else:
                        k.wait("pv", st, i, 2, p - 2)
                    b = bank[5 if kind == "dsa" else 4]
                    k.inc("ahi", eng.activation(a_hi[:, p, :], b[:, p * T:(p + 1) * T], ACT.Copy))

                def latent(i, p):
                    k.wait("pv", st, i, 2, p - 2)
                    k.wait("olc", st, i, 2, p - 3)
                    k.inc("ol", eng.activation(OL, bank[4][:, :].rearrange("p (a t) -> p a t", a=2), ACT.Copy))

                def evac(name, dst, b, sc=1.0):
                    return k.inc(name, eng.activation(dst, b[:, :].rearrange("p (a t) -> p a t", a=2), ACT.Copy,
                                                      scale=sc))

                def load_bias(i):
                    if not isinstance(i, int) or i > 0:
                        k.wait("lg", st, i, 4, -1)
                    src = biases[:, 0:4, :] if isinstance(i, int) else biases[:, bass.ds(i * 4, 4), :]
                    eng.dma_start(bias, src).then_inc(s_bias, 16)

                def body(i, loop, a, b, more):
                    split(st, i, a, b, loop)
                    done(st, i, a, b, loop)
                    if more:
                        k.wait("sc", st, i, 4, -1)
                    evac("qev", Q[:, 0:2, :], bank[4], 0.125 if kind == "sb" else 1.0)
                    if kind == "dsa":
                        k.wait("qev", st, i, 1, 0)
                        k.inc("qsq", eng.activation(qsq[0], mix[:, 0:512], ACT.Square))
                    split(st, i, a, b + 1, loop)
                    if more:
                        pt(i, 0)
                        pt(i, 1)
                    done(st, i, a, b + 1, loop)
                    if kind == "dsa":
                        evac("qev2", Q[:, 2:4, :], bank[5])
                        k.wait("qev2", st, i, 1, 0)
                        if isinstance(i, int):
                            k.wait("isc", st, b=8)
                        k.inc("qsq", eng.activation(qsq[1], mix[:, 512:1024], ACT.Square))
                        if more:
                            latent(i, 0)
                            pt(i, 2)
                            pt(i, 3)
                            out_hi(i, 0, loop)
                            latent(i, 1)
                            out_hi(i, 1, loop)
                            split(st, i, a, b + 2, loop)
                            k.wait("olc", st, i, 2, -1)
                        k.inc("wu", eng.activation(wu, par_("wuv", i * 256, 256), ACT.Copy))
                        k.wait("qss", st, i, 1, 0)
                        rs(rq, bank[7][:, 0:8], 1.0, eps128_c, ("qlr", "qlr"), st, i, 2, 0)
                    else:
                        evac("kev", KB, bank[5])
                        split(st, i, a, b + 2, loop)
                        if more:
                            out_hi(i, 0, loop)
                            pt(i, 2)
                            pt(i, 3)
                            out_hi(i, 1, loop)
                        done(st, i, a, b + 2, loop)
                        evac("vev", VB, bank[5])
                        if more:
                            split(st, i, a, b + 3, loop)
                    for h in range(5):
                        if h < 4:
                            softmax(i, h)
                        if h:
                            normalise(i, h - 1)

                if kind == "dsa":
                    sparse_front(st)
                    load_bias(0)
                    body(0, None, 0, 3, False)
                    for i in k.loop(1, n):
                        load_bias(i)
                        body(i, (1, n), 3, 2, True)
                else:
                    body(0, None, 0, 0, False)
                    for i in k.loop(1, n):
                        body(i, (1, n), 4, -1, True)
                pt(n, 0)
                pt(n, 1)
                if kind == "dsa":
                    latent(n, 0)
                    pt(n, 2)
                    pt(n, 3)
                    out_hi(n, 0, None)
                    latent(n, 1)
                    out_hi(n, 1, None)
                else:
                    out_hi(n, 0, None)
                    pt(n, 2)
                    pt(n, 3)
                    out_hi(n, 1, None)
                split(st, 0, 0, NBLK[kind] - 1)

            def sparse_front(st):
                two = dict(a=2)
                split(st, b=0)
                done(st, 0, 0, 0, None)
                eng.activation(latT, bank[4][:, 0:T], ACT.Copy)
                k.inc("pre", eng.activation(ki2, bank[4][:, T:2 * T], ACT.Copy))
                k.wait("pre", st, b=0)
                k.inc("ksq", eng.activation(qsq[0][:, 0:T], latT, ACT.Square))
                k.wait("relv", st)
                eng.dma_start(scratch, relS).then_inc(s_rel, 16)
                split(st, b=1)
                done(st, 0, 0, 1, None)
                k.inc("pre", eng.activation(Q[:, 0:2, :], bank[5][:, :].rearrange("p (a t) -> p a t", **two), ACT.Copy))
                k.wait("kss", st)
                rs(rstd[:, :], bank[7][:, 0:T], 1.0 / P, eps_c, ("klr", "klr"), st)
                split(st, b=2)
                eng.wait_ge(s_rel, 16)
                eng.dma_start(biases.rearrange("p h c -> h p c"),
                              bass.AP(scratch.tensor, 127, [[384, 16], [-1, P], [1, T]])).then_inc(s_rel, 16)
                done(st, 0, 0, 2, None)
                k.inc("pre", eng.activation(Q[:, 2:4, :], bank[6][:, :].rearrange("p (a t) -> p a t", **two), ACT.Copy))
                for h in range(8):
                    k.wait("ix", st, b=h)
                    if h >= 2:
                        k.wait("isc", st, b=h - 1)
                    k.inc("rel", eng.activation(R[:, h % 2, :], bank[4 + h % 2][:, 0:384], ACT.Relu))
                k.wait("ltp", st)
                k.inc("ltc", eng.activation(ltok, bank[7][:, 0:T].rearrange("p (a t) -> p a t", **two), ACT.Copy))
                eng.wait_ge(s_rel, 32)

            programs = {"ffn": ffn, "cffn": cffn, "mamba": mamba, "moba": lambda st: heads(st, "moba"),
                        "sb": lambda st: heads(st, "sb"), "dsa": lambda st: heads(st, "dsa")}
            for st, kind in enumerate(stages):
                norm(st)
                if kind in ("ffn", "cffn"):
                    eng.preload_act_table_set(SILU)
                programs[kind](st)

        @block.vector
        def _(eng):
            k = Steps(eng, plan, sems)
            eng.memset(eps_c, EPS)
            eng.memset(eps128_c, EPS * P)
            eng.memset(one_c, 1.0)
            eng.memset(zero_b, 0.0)

            def more_constants():
                eng.wait_ge(s_con, 16)
                eng.tensor_scalar(below_b, con_("tri"), 1.0, -NEG, ALU.subtract, ALU.mult).then_inc(sems["xst"], 1)
                eng.wait_ge(sems["const"], 1)
                eng.tensor_tensor(ws_lo[:, :], par_("wsmall"), ws_hi[:, :], ALU.subtract).then_inc(sems["xst"], 1)

            def split(st, i=0, a=0, b=0, it=None):
                blk = k.block(st, i, a, b + AHEAD, it)
                if blk is None:
                    return
                g, s, _ = blk
                eng.wait_ge(sems["whi"], g + 1)
                eng.tensor_tensor(w_lo[s][:, :], raw[s][:, :], w_hi[s][:, :], ALU.subtract).then_inc(sems["wlo"], 1)

            def fold(st, n):
                if st >= NST:
                    return
                if n == 0:
                    eng.wait_ge(sems["macc"] if st else sems["mo"], 31 * st or KT)
                half, w = n // 2, 1536 if st else 1024
                c, f = slice(w * half, w * half + w), slice(w // 32 * half, w // 32 * (half + 1))
                if n % 2 == 0:
                    k.inc("fold", eng.transpose(modws[:, c], macc[:, c]))
                else:
                    k.wait("fold", st, b=n - 1)
                    k.inc("fold", eng.tensor_reduce(folded[:, f], modws[:, c].rearrange("p (b c) -> p b c", c=32),
                                                    AX.X, ALU.add))

            def first_gate(rnd):
                eng.wait_ge(s_gate, 64 * (rnd + 1))
                for n in range(4 * rnd, 4 * rnd + 4):
                    if n == 0:
                        ins = eng.tensor_scalar(gacc, gatew[:, 0, :], cact[:, 0:1], None, ALU.mult)
                    else:
                        eng.wait_ge(sems["go"], n)
                        ins = eng.scalar_tensor_tensor(out=gacc, in0=gatew[:, n % 4, :], scalar=cact[:, n:n + 1],
                                                       in1=gacc, op0=ALU.mult, op1=ALU.add)
                    ins.then_inc(sems["go"], 1)
                if rnd:
                    eng.wait_ge(sems["go"], KT)
                    eng.transpose(gtr, gacc).then_inc(sems["go"], 1)
                    eng.wait_ge(sems["go"], KT + 1)
                    eng.tensor_reduce(gfold, gtr.rearrange("p (b c) -> p b c", c=32), AX.X,
                                      ALU.add).then_inc(sems["go"], 1)

            def tiles(st, c0, c1, at):
                sums = bank[7][:, at:at + 4 * (c1 - c0)].rearrange("p (c j) -> p c j", j=4)
                for j in range(4):
                    r = slice(32 * j, 32 * j + 32)
                    ins = eng.tensor_tensor(modv[r, st, c0:c1], sums[r, :, j],
                                            par_("modb", 24 * st + c0, c1 - c0)[r, :], ALU.add)
                return ins

            def modulation(st):
                k.wait("mods", st)
                mv = modv[:, st, :]
                ins = tiles(st, 0, 24 if st else 16, 0)
                ins.then_inc(sems["xst"], 1)
                eng.wait_ge(sems["xst"], 2 + 2 * st + 1)
                if st and stages[st] == "ffn":
                    eng.tensor_scalar(mv[:, 16:24], mv[:, 16:24], 0.5, None, ALU.mult)
                eng.tensor_scalar(gs[:, st, :], mv[:, 8:16], 1.0, None, ALU.add).then_inc(sems["xst"], 1)
                eng.wait_ge(sems["xst"], 2 + 2 * st + 2)
                k.inc("modv", eng.tensor_tensor(gs[:, st, :], gs[:, st, :], par_("g", 8 * st, 8), ALU.mult))

            def norm(st):
                final = st == RESCALED
                k.wait("rstd", st)
                r = rstd[:, :]
                if final:
                    k.inc("ms2", eng.tensor_tensor(rstd2, rstd[:, :], rstd[:, :], ALU.mult))
                    k.wait("ms2", st)
                    k.inc("ms2", eng.tensor_tensor(rstd2, rstd2, bank[6][:, T:2 * T], ALU.mult))
                    k.inc("ms2", eng.tensor_tensor(gs[:, st, :], gs[:, st, :], par_("gfin"), ALU.mult))
                    k.wait("rstd", st, b=1)
                    k.wait("ms2", st, b=2)
                    r = rstd2
                    k.inc("ms2", eng.tensor_tensor(r, r, rstd[:, :], ALU.mult))
                    k.wait("ms2", st, b=3)
                k.wait("modv", st)
                for m in range(KT):
                    k.inc("t", eng.scalar_tensor_tensor(out=work3[:, m, :], in0=x[:, m, :],
                                                        scalar=gs[:, st, m:m + 1], in1=r,
                                                        op0=ALU.mult, op1=ALU.mult))
                for m in range(KT):
                    k.wait("hhi", st, b=m)
                    k.inc("hlo", eng.scalar_tensor_tensor(
                        out=h_lo[:, m, :], in0=work3[:, m, :], scalar=modv[:, st, m:m + 1],
                        in1=h_hi[:, m, :], op0=ALU.add, op1=ALU.subtract))
                if final:
                    for m in range(KT):
                        k.inc("xfin", eng.scalar_tensor_tensor(
                            out=x[:, m, :], in0=x[:, m, :], scalar=par_("gfin", m, 1), in1=rstd[:, :],
                            op0=ALU.mult, op1=ALU.mult))
                if st == 0:
                    split(0, b=-1)

            def residual(st):
                if st == 0:
                    eng.wait_ge(sems["gmods"], 1)
                    tiles(0, 16, 24, 96).then_inc(sems["go"], 1)
                    eng.wait_ge(sems["go"], KT + 3)
                    eng.tensor_scalar(modv[:, 0, 16:24], modv[:, 0, 16:24], 0.5, None,
                                      ALU.mult).then_inc(sems["go"], 1)
                    eng.wait_ge(sems["go"], KT + 4)
                token = stages[st] == "mamba"
                if token:
                    k.wait("rs2", st, b=1)
                for pair in range(4):
                    if pair == 2:
                        split(st, b=NBLK[stages[st]] - 1)
                    if pair < 3:
                        k.wait("pair", st, b=pair)
                    else:
                        eng.wait_ge(sems["blk"], plan.first[st] + NBLK[stages[st]])
                    two = (2 * pair, 2 * pair + 1)
                    if token:
                        for m in two:
                            k.inc("xr", eng.tensor_tensor(work3[:, m, :], acc(m), r2, ALU.mult))
                    for m in two:
                        if token:
                            k.wait("xr", st, b=m)
                        k.inc("xup", eng.scalar_tensor_tensor(
                            out=x[:, m, :], in0=work3[:, m, :] if token else acc(m),
                            scalar=modv[:, st, 16 + m:17 + m], in1=x[:, m, :], op0=ALU.mult, op1=ALU.add))

            def ffn(st):
                def gate(i, a, b, loop):
                    split(st, i, a, b, loop)

                def up(i, a, b, loop):
                    split(st, i, a, b, loop)
                    eng.wait_ge(sems["blk"], k.block(st, i, a, b, loop)[0] + 1)
                    k.wait("silu", st, i, 1, 0)
                    k.wait("alo", st, i, 1, -1)
                    k.inc("mul", eng.tensor_tensor(act, sg, bank[5][:, :].rearrange("p (a t) -> p a t", a=2),
                                                   ALU.mult))

                def lo(i):
                    final = isinstance(i, int) and i == NFB - 1
                    k.wait("ahi", st, i, 1, 0)
                    k.inc("alo", eng.tensor_tensor(z_lo if final else a_lo[:, :, :], act,
                                                   z_hi if final else a_hi[:, :, :], ALU.subtract))

                def down(i, a, b, loop):
                    split(st, i, a, b, loop)
                    lo(i)

                gate(0, 0, 0, None)
                up(0, 0, 1, None)
                lo(0)
                begin = 1
                if st == 0:
                    for n in range(1, GATE_AT + 5):
                        gate(n, 3, -1, None)
                        up(n, 3, 0, None)
                        if n in (GATE_AT, GATE_AT + 4):
                            first_gate((n - GATE_AT) // 4)
                        down(n, 3, 1, None)
                    begin = GATE_AT + 5
                for i in k.loop(begin, FOLD_AT):
                    part = (begin, FOLD_AT)
                    gate(i, 3, -1, part)
                    up(i, 3, 0, part)
                    down(i, 3, 1, part)
                for n in range(FOLD_AT, NFB):
                    steps = (0, 1, 2, 3) if n == FOLD_AT else ()
                    gate(n, 3, -1, None)
                    for step in steps[:2]:
                        fold(st + 1, step)
                    up(n, 3, 0, None)
                    for step in steps[2:3]:
                        fold(st + 1, step)
                    down(n, 3, 1, None)
                    for step in steps[3:]:
                        fold(st + 1, step)

            def cffn(st):
                ci = sum(1 for z in stages[:st] if z == "cffn")

                def cw(i, tile, tap):
                    if isinstance(i, int):
                        return par_("fcw", ((ci * 44 + 2 * i + tile) * 4) + tap, 1)
                    return par_("fcw", i * 8 + (ci * 44 + tile) * 4 + tap, 1)

                def taps(i, up):
                    b, dst = bank[5 if up else 4], cu if up else cg
                    k.wait("cid", st, i, 2, up)
                    for tap, name in ((1, "tap1"), (0, "tap2")):
                        lag = 2 - tap
                        if tap == 0:
                            k.wait("tap1", st, i, 2, up)
                        for m in range(2):
                            ins = eng.scalar_tensor_tensor(
                                out=dst[:, m, lag:T], in0=b[:, m * T:(m + 1) * T - lag],
                                scalar=cw(i, 22 * up + m, tap), in1=dst[:, m, lag:T], op0=ALU.mult, op1=ALU.add)
                        k.inc(name, ins)

                def gate(i, a, b, loop):
                    split(st, i, a, b, loop)
                    taps(i, 0)

                def up(i, a, b, loop):
                    split(st, i, a, b, loop)
                    taps(i, 1)
                    k.wait("silu", st, i, 1, 0)
                    k.wait("alo", st, i, 1, -1)
                    k.wait("tap2", st, i, 2, 1)
                    k.inc("mul", eng.tensor_tensor(act, sg, cu, ALU.mult))

                def lo(i):
                    final = isinstance(i, int) and i == NFB - 1
                    k.wait("ahi", st, i, 1, 0)
                    k.inc("alo", eng.tensor_tensor(z_lo if final else a_lo[:, :, :], act,
                                                   z_hi if final else a_hi[:, :, :], ALU.subtract))

                def down(i, a, b, loop):
                    split(st, i, a, b, loop)
                    lo(i)

                gate(0, 0, 0, None)
                up(0, 0, 1, None)
                lo(0)
                for i in k.loop(1, FOLD_AT):
                    part = (1, FOLD_AT)
                    gate(i, 3, -1, part)
                    up(i, 3, 0, part)
                    down(i, 3, 1, part)
                for n in range(FOLD_AT, NFB):
                    steps = (0, 1, 2, 3) if n == FOLD_AT else ()
                    gate(n, 3, -1, None)
                    for step in steps[:2]:
                        fold(st + 1, step)
                    up(n, 3, 0, None)
                    for step in steps[2:3]:
                        fold(st + 1, step)
                    down(n, 3, 1, None)
                    for step in steps[3:]:
                        fold(st + 1, step)

            def mamba(st):
                two = dict(a=2)
                k.inc("sq0", eng.memset(sqa, 0.0))
                step = [0]

                def timestep():
                    k.wait("dtp", st)

                    def dt_step(ins, wait=True):
                        k.inc("dta", ins)
                        step[0] += 1
                        if wait:
                            k.wait("dta", st, b=step[0] - 1)

                    dt_step(eng.tensor_tensor(dv.rearrange("p (a h) -> p a h", a=2),
                                              bank[6][:, 0:64].rearrange("p (a h) -> p a h", a=2),
                                              par_("dtb").unsqueeze(1).to_broadcast([P, 2, 32]), ALU.add), False)
                    k.wait("dtx", st, b=1)
                    dt_step(eng.tensor_scalar(dw, de, 1.0, None, ALU.add))
                    k.wait("dtx", st, b=2)
                    dt_step(eng.tensor_scalar(dw, dw, 1.0, None, ALU.subtract))
                    dt_step(eng.tensor_scalar(dm, dw, 0.0, None, ALU.is_equal))
                    dt_step(eng.tensor_tensor(dw, dw, dm, ALU.add))
                    dt_step(eng.reciprocal(dw, dw))
                    dt_step(eng.tensor_tensor(dl, dl, dm, ALU.add))
                    dt_step(eng.tensor_tensor(dl, dl, dw, ALU.mult))
                    dt_step(eng.tensor_tensor(dl, dl, de, ALU.mult))
                    dt_step(eng.scalar_tensor_tensor(out=dtt, in0=dv, scalar=0.0, in1=dl, op0=ALU.max, op1=ALU.add))
                    k.wait("dtx", st, b=3)
                    for d in range(2):
                        dt_step(eng.scalar_tensor_tensor(
                            out=dta[:, :, d, :], in0=dtt.rearrange("p (a h) -> p a h", a=2),
                            scalar=-1.0, in1=ea.unsqueeze(1).to_broadcast([P, 2, 32]), op0=ALU.mult, op1=ALU.mult), False)

                dt3 = dtt.rearrange("p (a h) -> p a h", a=2)

                def cum():
                    k.wait("acp", st)
                    k.inc("acv", eng.tensor_scalar(nac, bank[6][:, T:T + 64], -1.0, None, ALU.mult))
                    eng.tensor_copy(acg[:, 0:T], bank[6][0:64, 0:T])
                    k.inc("acv", eng.tensor_copy(acg[:, T:384], bank[6][0:64, P:T]))
                    k.wait("acv", st, b=1)
                    eng.tensor_copy(acT[0:32, :], acg[0:32, :])
                    lo = slice(32, 64)
                    eng.tensor_tensor(acT[lo, 0:T], bank[6][lo, 0:T], acg[lo, 0:T], ALU.subtract)
                    k.inc("acv", eng.tensor_tensor(acT[lo, T:384], bank[6][lo, P:T], acg[lo, T:384], ALU.subtract))

                def taps(i, which, dst, b):
                    k.wait("cid", st, i, 2, which)
                    for n, tap in enumerate((2, 1, 0)):
                        lag = 3 - tap
                        if n:
                            k.wait("tap", st, i, 6, 3 * which + n - 1)
                        for m in range(2):
                            ins = eng.scalar_tensor_tensor(
                                out=dst[:, m, lag:T], in0=b[:, m * T:(m + 1) * T - lag],
                                scalar=par_("cw", i * 20 + (2 * which + m) * 5 + tap, 1),
                                in1=dst[:, m, lag:T], op0=ALU.mult, op1=ALU.add)
                        k.inc("tap", ins)

                def weigh(i, off, h):
                    k.wait("dec", st, i, 4, 4 * off + h)
                    if h == 0:
                        k.wait("cbs", st, i, 1, off)
                    k.inc("wv", eng.tensor_tensor(S[:, h, :], S[:, h, :], cbs, ALU.mult))

                def y_parts(i):
                    k.wait("yc", st, i, 1, -1)
                    k.inc("y1", eng.tensor_tensor(yb, bank[6][:, :].rearrange("p (a t) -> p a t", **two), dx, ALU.add))
                    k.wait("y1", st, i, 1, -1)
                    k.wait("zw", st, i, 1, -1)
                    k.inc("yn", eng.tensor_tensor(yn, yb, yn, ALU.mult))
                    k.wait("yn", st, i, 1, -1)
                    k.inc("yz", eng.tensor_tensor(yb, yb, zc, ALU.mult))

                def gate_z(i):
                    k.wait("sil", st, i, 3, -1)
                    k.wait("alo", st, i, 1, -2)
                    for m in range(2):
                        ins = eng.tensor_scalar(yn[:, m, :], zc[:, m, :], par_("ngw", i * 2 + (m - 2), 1), None,
                                                ALU.mult)
                    k.inc("zw", ins)

                def y_squares(i):
                    k.wait("ysq", st, i, 1, -1)
                    k.wait("sq0", st)
                    k.wait("yac", st, i, 1, -2)
                    k.inc("yac", eng.tensor_tensor(sqa, sqa, sqt, ALU.add))

                def lo(i):
                    k.wait("ahi", st, i, 1, -1)
                    k.inc("alo", eng.tensor_tensor(a_lo[:, :, :], yn, a_hi[:, :, :], ALU.subtract))

                def group_rows(i):
                    gm = CONSTS["gmask"][0]
                    col = con[0:64, gm + i:gm + i + 1] if isinstance(i, int) else con[0:64, bass.ds(i + gm, 1)]
                    k.inc("acg", eng.tensor_scalar(acg, acT, col, None, ALU.mult))

                def body(i, loop, a, b, final=False):
                    more = not isinstance(i, int) or i > 0
                    split(st, i, a, b, loop)
                    taps(i, 0, xc, bank[4])
                    if more:
                        gate_z(i)
                        weigh(i, -1, 2)
                        weigh(i, -1, 3)
                    else:
                        timestep()
                    split(st, i, a, b + 1, loop)
                    if final:
                        fold(st + 1, 0)
                    taps(i, 1, bc, bank[5])
                    if more:
                        k.wait("br", st, i, 4, -1)
                        group_rows(i)
                    if more:
                        y_parts(i)
                        lo(i)
                    else:
                        cum()
                        k.wait("acv", st, b=2)
                        group_rows(i)
                    k.wait("xt", st, i, 1, 0)
                    heads4 = dt3[:, :, 4 * i:4 * i + 4] if isinstance(i, int) else dt3[:, :, bass.ds(i * 4, 4)]
                    k.inc("xdt", eng.tensor_tensor(
                        xdt.rearrange("p a (h c) -> p a h c", h=4),
                        bank[4][:, :].rearrange("p (a h c) -> p a h c", a=2, h=4),
                        heads4.unsqueeze(3).to_broadcast([P, 2, 4, HD]), ALU.mult))
                    k.wait("cb", st, i, 1, 0)
                    k.inc("cbs", eng.tensor_copy(cbs, bank[5][:, 0:384]))
                    split(st, i, a, b + 2, loop)
                    if final:
                        fold(st + 1, 1)
                    if more:
                        y_squares(i)
                        split(st, i, a, b + 3, loop)
                    if final:
                        fold(st + 1, 2)
                        fold(st + 1, 3)
                    for m in range(2):
                        ins = eng.tensor_scalar(dx[:, m, :], xc[:, m, :], par_("dskip", i * 2 + m, 1), None, ALU.mult)
                    k.inc("dx", ins)
                    weigh(i, 0, 0)
                    weigh(i, 0, 1)

                n = GROUPS["mamba"]
                body(0, None, 0, 0)
                at = n - 3
                for i in k.loop(1, at):
                    body(i, (1, at), 4, -1)
                body(at, None, 4, -1, True)
                for i in k.loop(at + 1, n):
                    body(i, (at + 1, n), 4, -1)
                gate_z(n)
                weigh(n, -1, 2)
                weigh(n, -1, 3)
                y_parts(n)
                lo(n)
                y_squares(n)

            def heads(st, kind):
                n = GROUPS[kind]
                scale = 0.125 if kind == "moba" else 1.0

                def softmax(i, h):
                    k.wait("sc", st, i, 4, h)
                    b = bank[4 + h]
                    if kind == "moba":
                        sl = CONSTS["slope8"][0]
                        col = con[:, sl + 4 * i + h:sl + 4 * i + h + 1] if isinstance(i, int) else \
                            con[:, bass.ds(i * 4 + (sl + h), 1)]
                        k.inc("lg", eng.scalar_tensor_tensor(out=S[:, h, :], in0=con_("dist"), scalar=col,
                                                             in1=b[:, 0:384], op0=ALU.mult, op1=ALU.add))
                    elif kind == "dsa":
                        if h == 0:
                            k.wait("qlr", st, i, 2, 1)
                            base = plan.base["lg"][st] // 4
                            eng.wait_ge(s_bias, i * 16 + 16)
                        for c0, c1, tt, bb in ((0, 128, 0, 128), (128, 384, 1, 0)):
                            ins = eng.scalar_tensor_tensor(
                                out=S[:, h, c0:c1], in0=b[:, c0:c1], scalar=rq[:, 2 * h + tt:2 * h + tt + 1],
                                in1=bias[:, h, bb:bb + c1 - c0], op0=ALU.mult, op1=ALU.add)
                        k.inc("lg", ins)
                    else:
                        k.inc("lg", eng.tensor_copy(S[:, h, :], b[:, 0:384]))
                        return
                    k.wait("lg", st, i, 4, h)
                    eng.tensor_reduce(mxt[:, 2 * h:2 * h + 1], S[:, h, 0:128], AX.X, ALU.max)
                    k.inc("mx", eng.tensor_reduce(mxt[:, 2 * h + 1:2 * h + 2], S[:, h, 128:384], AX.X, ALU.max))
                    k.wait("mx", st, i, 4, h)
                    k.inc("nm", eng.tensor_scalar(nmx[:, 2 * h:2 * h + 2], mxt[:, 2 * h:2 * h + 2], -scale, None,
                                                  ALU.mult))

                def finish(i, h):
                    if kind == "sb":
                        k.wait("la", st, i, 4, h)
                        k.inc("lk", eng.scalar_tensor_tensor(out=LK[:, h, :], in0=S[:, h, :], scalar=0.0,
                                                             in1=LK[:, h, :], op0=ALU.max, op1=ALU.add))
                        k.wait("lk", st, i, 4, h)
                        for c in (0, 256):
                            ins = eng.tensor_tensor(LK[:, h, c:c + P], LK[:, h, c:c + P], con_("strict"), ALU.mult)
                        k.inc("prb", ins)
                        return
                    k.wait("ex", st, i, 4, h)
                    k.inc("rc", eng.reciprocal(rcp[:, 2 * h:2 * h + 2], sums[:, 2 * h:2 * h + 2]))

                def arg(i, h):
                    if kind == "sb":
                        k.wait("ptp", st, i, 4, h - 4)
                        k.inc("arg", eng.tensor_tensor(S[:, h, :], S[:, h, :], bank[7 - h % 2][:, 0:384], ALU.subtract))

                def out_lo(i, p):
                    k.wait("ahi", st, i, 2, p - 2)
                    b = bank[5 if kind == "dsa" else 4]
                    k.inc("alo", eng.tensor_tensor(a_lo[:, p, :], b[:, p * T:(p + 1) * T], a_hi[:, p, :],
                                                   ALU.subtract))

                def body(i, loop, a, b, more, final=False):
                    split(st, i, a, b, loop)
                    if final:
                        fold(st + 1, 0)
                        fold(st + 1, 1)
                    split(st, i, a, b + 1, loop)
                    if more:
                        arg(i, 0)
                        arg(i, 1)
                    if final:
                        fold(st + 1, 2)
                    if kind == "dsa":
                        if more:
                            out_lo(i, 0)
                            out_lo(i, 1)
                            split(st, i, a, b + 2, loop)
                            if final:
                                fold(st + 1, 3)
                    else:
                        split(st, i, a, b + 2, loop)
                        if more:
                            out_lo(i, 0)
                            arg(i, 2)
                            arg(i, 3)
                            if final:
                                fold(st + 1, 3)
                            out_lo(i, 1)
                            split(st, i, a, b + 3, loop)
                    softmax(i, 0)
                    for h in range(4):
                        if h < 3:
                            softmax(i, h + 1)
                        finish(i, h)

                if kind == "dsa":
                    sparse_front(st)
                    body(0, None, 0, 3, False)
                    for i in k.loop(1, n - 1):
                        body(i, (1, n - 1), 3, 2, True)
                    body(n - 1, None, 3, 2, True, True)
                else:
                    body(0, None, 0, 0, False)
                    for i in k.loop(1, n - 1):
                        body(i, (1, n - 1), 4, -1, True)
                    body(n - 1, None, 4, -1, True, True)
                arg(n, 0)
                arg(n, 1)
                out_lo(n, 0)
                arg(n, 2)
                arg(n, 3)
                out_lo(n, 1)

            def sparse_front(st):
                split(st, b=0)
                k.wait("relp", st)
                k.inc("wiv", eng.tensor_scalar(wi, bank[7][:, 0:16].rearrange("p (a h) -> p a h", a=2), 8 ** -0.5,
                                               None, ALU.mult))
                k.inc("relv", eng.tensor_copy(relS, bank[7][0:16, P:512]))
                k.inc("gkq", eng.tensor_tensor(gkq, par_("qn"), par_("kn"), ALU.mult))
                k.inc("isc", eng.memset(isc, 0.0))
                split(st, b=1)
                k.wait("gkq", st)
                k.wait("klr", st, b=1)
                k.inc("kn", eng.scalar_tensor_tensor(out=kn, in0=latT, scalar=gkq, in1=rstd[:, :],
                                                     op0=ALU.mult, op1=ALU.mult))
                split(st, b=2)
                k.wait("wiv", st)
                for h in range(8):
                    k.wait("rel", st, b=h)
                    k.wait("isc", st, b=h)
                    for c0, c1, tt in ((0, 128, 0), (128, 384, 1)):
                        ins = eng.scalar_tensor_tensor(out=isc[:, c0:c1], in0=R[:, h % 2, c0:c1],
                                                       scalar=wi[:, tt, h:h + 1], in1=isc[:, c0:c1],
                                                       op0=ALU.mult, op1=ALU.add)
                    k.inc("isc", ins)
                k.wait("isc", st, b=8)
                k.inc("isc", eng.tensor_tensor(isc, isc, con_("causal"), ALU.add))
                k.wait("isc", st, b=9)
                for r in range(8):
                    for tt, (c0, c1) in enumerate(((0, 128), (128, 384))):
                        if r:
                            k.wait("top", st, b=4 * r - 2 + tt)
                        k.inc("top", eng.max(v8[tt], (wk if r else isc)[:, c0:c1]))
                    for tt, (c0, c1) in enumerate(((0, 128), (128, 384))):
                        k.wait("top", st, b=4 * r + tt)
                        k.inc("top", eng.match_replace(wk[:, c0:c1], v8[tt], (wk if r else isc)[:, c0:c1], GONE))
                k.wait("top", st, b=31)
                k.inc("msk", eng.tensor_scalar(isc, wk, -2e38, NEG, ALU.is_gt, ALU.mult))
                k.wait("msk", st)
                k.inc("msk", eng.tensor_tensor(maskb, isc, con_("causal"), ALU.add))

            programs = {"ffn": ffn, "cffn": cffn, "mamba": mamba, "moba": lambda st: heads(st, "moba"),
                        "sb": lambda st: heads(st, "sb"), "dsa": lambda st: heads(st, "dsa")}
            eng.wait_ge(sems["cact"], 1)
            for n in range(KT):
                eng.wait_ge(s_mo[n % 4], 16 * (n // 4 + 1))
                if n == 0:
                    ins = eng.tensor_scalar(macc[:, 0:2048], first_mod[0], cact[:, 0:1], None, ALU.mult)
                else:
                    eng.wait_ge(sems["mo"], n)
                    ins = eng.scalar_tensor_tensor(out=macc[:, 0:2048], in0=first_mod[n % 4], scalar=cact[:, n:n + 1],
                                                   in1=macc[:, 0:2048], op0=ALU.mult, op1=ALU.add)
                ins.then_inc(sems["mo"], 1)
            for n in range(4):
                fold(0, n)
            more_constants()
            split(0, b=-2)
            modulation(0)
            for st, kind in enumerate(stages):
                norm(st)
                programs[kind](st)
                residual(st)
                if st + 1 < NST:
                    modulation(st + 1)

        @block.tensor
        def _(eng):
            k = Steps(eng, plan, sems)

            def begin(st, i, a, b, it):
                g, s, _ = k.block(st, i, a, b, it)
                eng.wait_ge(sems["wlo"], g + 1)
                hi = w_hi[s][:, :].rearrange("p (k n) -> p k n", k=KT)
                lo = w_lo[s][:, :].rearrange("p (k n) -> p k n", k=KT)
                return s, hi, lo

            def three(dst, ah, al, bh, bl, start, stop, skip=False):
                eng.matmul(dst, ah, bh, start=start, stop=False, skip_group_check=skip)
                eng.matmul(dst, ah, bl, start=False, stop=False, skip_group_check=skip)
                return eng.matmul(dst, al, bh, start=False, stop=stop, skip_group_check=skip)

            def gemm(dst, st, i=0, a=0, b=0, it=None, tokens=False, first=False):
                s, hi, lo = begin(st, i, a, b, it)
                both = [(m, slice(m * P, (m + 1) * P), dst[:, m * T:(m + 1) * T]) for m in range(2)]
                if first:
                    for kk in range(KT):
                        k.wait("hhi", st, b=kk)
                        for m, part, d in both:
                            eng.matmul(d, hi[:, kk, part], h_hi[:, kk, :], start=kk == m == 0, stop=False,
                                       skip_group_check=True)
                            eng.matmul(d, lo[:, kk, part], h_hi[:, kk, :], start=False, stop=False,
                                       skip_group_check=True)
                    for kk in range(KT):
                        k.wait("hlo", st, b=kk)
                        for m, part, d in both:
                            mm = eng.matmul(d, hi[:, kk, part], h_lo[:, kk, :], start=False, stop=kk == KT - 1,
                                            skip_group_check=True)
                else:
                    for m, part, d in both:
                        for kk in range(KT):
                            if tokens:
                                mm = three(d, h_hi[:, kk, part], h_lo[:, kk, part], hi[:, kk, :], lo[:, kk, :],
                                           kk == 0, kk == KT - 1)
                            else:
                                mm = three(d, hi[:, kk, part], lo[:, kk, part], h_hi[:, kk, :], h_lo[:, kk, :],
                                           kk == 0, kk == KT - 1)
                mm.then_inc(sems["blk"], 1)

            def gemm_out(st, i=0, a=0, b=0, it=None, ready=None):
                s, _, _ = begin(st, i, a, b, it)
                hi = w_hi[s][:, :].rearrange("p (k n) -> p k n", k=2)
                lo = w_lo[s][:, :].rearrange("p (k n) -> p k n", k=2)
                for kk in range(2):
                    ready(kk)
                    for m in range(KT):
                        part = slice(m * P, (m + 1) * P)
                        mm = three(acc(m), hi[:, kk, part], lo[:, kk, part], a_hi[:, kk, :], a_lo[:, kk, :],
                                   False, False, True)
                mm.then_inc(sems["blk"], 1)

            def modulation(st):
                k.wait("fold", st, b=3)
                if st:
                    k.wait("modv", st - 1)
                w = 96 if st else 64
                k.inc("mods", eng.matmul(bank[7][:, 0:w], con_("fold"), folded[:, 0:w], start=True, stop=True))

            def squares(st, pair):
                final = st == RESCALED
                for m in (2 * pair, 2 * pair + 1):
                    for r in range(2 if final else 1):
                        k.wait("sq", st, b=(2 * m + r) if final else m)
                        mm = eng.matmul(bank[6][:, r * T:(r + 1) * T], con_("ones"), (sq2 if r else work3)[:, m, :],
                                        start=m == r == 0, stop=m == KT - 1, skip_group_check=True)
                if pair == 3:
                    k.inc("ss", mm)

            def norm(st):
                if st == 0:
                    for pair in range(4):
                        squares(0, pair)
                    modulation(0)
                    eng.wait_ge(sems["const"], 1)
                    eng.wait_ge(sems["xst"], 2)
                else:
                    k.wait("xup", st - 1, b=7)
                for n in range(4):
                    mm = eng.matmul(bank[n][:, :].rearrange("p (a c) -> p a c", a=4), ident_b,
                                    zero_b.unsqueeze(1).to_broadcast([P, 4, P]), start=True, stop=True)
                k.inc("zero", mm)

            def ffn(st):
                kind = stages[st]
                free4, per4, free5, per5 = ("silu", 1, "mul", 1) if kind == "ffn" else ("tap2", 2, "tap2", 2)

                def gate(i, a, b, loop, first=False):
                    if not first:
                        k.wait(free4, st, i, per4, -per4)
                    gemm(bank[4], st, i, a, b, loop, first=first)

                def up(i, a, b, loop, first=False):
                    if not first:
                        k.wait(free5, st, i, per5, -1)
                    gemm(bank[5], st, i, a, b, loop)

                def down(i, a, b, loop):
                    gemm_out(st, i, a, b, loop, lambda kk: k.wait("alo", st, i, 1, -1) if kk == 0 else None)

                gate(0, 0, 0, None, True)
                up(0, 0, 1, None, True)
                for i in k.loop(1, NFB - 1):
                    r = (1, NFB - 1)
                    gate(i, 3, -1, r)
                    up(i, 3, 0, r)
                    down(i, 3, 1, r)
                n = NFB - 1
                gate(n, 3, -1, None)
                up(n, 3, 0, None)
                down(n, 3, 1, None)
                last(st, lambda: k.wait("alo", st, b=n))

            def last(st, ready):
                s, _, _ = begin(st, 0, 0, NBLK[stages[st]] - 1, None)
                hi = w_hi[s][:, :].rearrange("p (k n) -> p k n", k=2)
                lo = w_lo[s][:, :].rearrange("p (k n) -> p k n", k=2)
                ready()
                ffn = stages[st] in ("ffn", "cffn")
                ahi, alo = (z_hi, z_lo) if ffn else (a_hi, a_lo)
                more = st + 1 < NST
                if st == 0:
                    eng.wait_ge(sems["go"], KT + 2)
                    eng.matmul(bank[7][:, 96:128], con_("fold"), gfold, start=True,
                               stop=True).then_inc(sems["gmods"], 1)
                for pair in range(4):
                    if pair == 3 and more:
                        squares(st + 1, 0)
                    for m in (2 * pair, 2 * pair + 1):
                        part = slice(m * P, (m + 1) * P)
                        for kk in range(2):
                            mm = three(acc(m), hi[:, kk, part], lo[:, kk, part], ahi[:, kk, :], alo[:, kk, :],
                                       False, False, True)
                    if pair < 3:
                        k.inc("pair", mm)
                    else:
                        mm.then_inc(sems["blk"], 1)
                if more:
                    squares(st + 1, 1)
                    modulation(st + 1)
                    squares(st + 1, 2)
                    squares(st + 1, 3)

            def mamba(st):
                def timestep():
                    k.wait("rstd", st)
                    for tt in range(2):
                        for kk in range(KT):
                            part = slice(tt * P, (tt + 1) * P)
                            ws = slice(40 * kk, 40 * kk + 32)
                            mm = three(bank[6][:, 32 * tt:32 * tt + 32], h_hi[:, kk, part], h_lo[:, kk, part],
                                       ws_hi[:, ws], ws_lo[:, ws], kk == 0, kk == KT - 1)
                    k.inc("dtp", mm)

                tri, ones = con_("tri"), con_("ones")

                def cum():
                    k.wait("dta", st, b=11)
                    d0, d1 = dta[:, 0, 0, :], dta[:, 1, 0, :]
                    eng.matmul(bank[6][:, T:T + 32], tri, d0, start=True, stop=True)
                    eng.matmul(bank[6][:, T + 32:T + 64], ones, d0, start=True, stop=False)
                    eng.matmul(bank[6][:, T + 32:T + 64], tri, d1, start=False, stop=True)
                    d0, d1 = (dta[:, tt, :, :].rearrange("p d h -> p (d h)") for tt in range(2))
                    eng.matmul(bank[6][0:64, 0:P], d0, tri, start=True, stop=True)
                    eng.matmul(bank[6][0:64, P:T], d0, ones, start=True, stop=False)
                    k.inc("acp", eng.matmul(bank[6][0:64, P:T], d1, tri, start=False, stop=True))

                def rows(i, off, h, free):
                    free()
                    b = bank[6 + h % 2]
                    eng.matmul(b[:, 0:384], sel[:, h * P:(h + 1) * P], acg, start=True, stop=False,
                               skip_group_check=True)
                    diag = b[:, :].rearrange("p (a b c) -> p a b c", a=2, b=2)[:, :, 0, :]
                    k.inc("br", eng.matmul(diag, ident_b, below_b.unsqueeze(1).to_broadcast([P, 2, P]),
                                           start=False, stop=True, skip_group_check=True))

                def parts(i):
                    k.wait("sil", st, i, 3, 0)
                    for m in range(2):
                        for tt in range(2):
                            mm = eng.transpose(bank[4][:, tt * T + m * P:tt * T + (m + 1) * P],
                                               xc[:, m, tt * P:(tt + 1) * P], con_("ident"))
                    k.inc("xt", mm)
                    k.wait("sil", st, i, 3, 1)
                    eng.matmul(bank[5][:, 0:T], bc[:, 0, 0:P], bc[:, 1, :], start=True, stop=True)
                    k.inc("cb", eng.matmul(bank[5][:, T:384], bc[:, 0, P:T], bc[:, 1, P:T], start=True, stop=True))

                def first_rows(i):
                    if isinstance(i, int):
                        k.wait("acv", st, b=2)
                    k.wait("acg", st, i, 1, 0)
                    rows(i, 0, 0, lambda: k.wait("y1", st, i, 1, -1))
                    rows(i, 0, 1, lambda: k.wait("sil", st, i, 3, 2))

                def more_rows(i):
                    rows(i, -1, 2, lambda: k.wait("dec", st, i, 4, -4))
                    rows(i, -1, 3, lambda: k.wait("dec", st, i, 4, -3))

                def y_out(i):
                    k.wait("dec", st, i, 4, -2)
                    k.wait("xdt", st, i, 1, -1)
                    for h in range(4):
                        k.wait("wv", st, i, 4, h - 4)
                        rows_, c0 = slice(HD * (h % 2), HD * (h % 2) + HD), (h // 2) * T
                        ch = slice(h * HD, (h + 1) * HD)
                        eng.matmul(bank[6][rows_, c0:c0 + T], xdt[:, 0, ch], S[:, h, 0:T], start=True, stop=False)
                        mm = eng.matmul(bank[6][rows_, c0 + P:c0 + T], xdt[:, 1, ch], S[:, h, T:384],
                                        start=False, stop=True)
                    k.inc("yc", mm)

                def body(i, loop, a, b):
                    more = not isinstance(i, int) or i > 0
                    k.wait("xdt", st, i, 1, -1)
                    gemm(bank[4], st, i, a, b, loop, first=not more)
                    if more:
                        more_rows(i)
                    else:
                        timestep()
                    k.wait("cbs", st, i, 1, -1)
                    gemm(bank[5], st, i, a, b + 1, loop)
                    if more:
                        y_out(i)
                        k.wait("dec", st, i, 4, -1)
                    gemm(bank[7], st, i, a, b + 2, loop)
                    if not more:
                        cum()
                    parts(i)
                    if more:
                        gemm_out(st, i, a, b + 3, loop, lambda kk: k.wait("alo", st, i, 1, -1) if kk == 0 else None)
                    first_rows(i)

                n = GROUPS["mamba"]
                body(0, None, 0, 0)
                for i in k.loop(1, n):
                    body(i, (1, n), 4, -1)
                more_rows(n)
                y_out(n)
                k.wait("yac", st, b=n - 1)
                eng.matmul(bank[6][:, 0:T], ones, sqa[:, 0, :], start=True, stop=False)
                k.inc("rs2p", eng.matmul(bank[6][:, 0:T], ones, sqa[:, 1, :], start=False, stop=True))
                k.wait("dec", st, b=4 * n - 1)
                last(st, lambda: k.wait("alo", st, b=n - 1))

            def heads(st, kind):
                n = GROUPS[kind]

                def scores(i):
                    free = {4: ("alo", 2, -1), 5: ("vev", 1, 0), 6: ("ptc", 4, -1), 7: ("ptc", 4, -2)}
                    if kind == "sb":
                        free[6], free[7] = ("arg", 4, -1), ("arg", 4, -2)
                    if kind == "dsa":
                        free[5] = ("alo", 2, -1)
                    k.wait("qev" if kind != "dsa" else "qev2", st, i, 1, 0)
                    if kind != "dsa":
                        k.wait("kev", st, i, 1, 0)
                    else:
                        k.wait(*free[7][:1], st, i, *free[7][1:])
                        for h in range(4):
                            if h % 2 == 0:
                                k.wait("qsq", st, i, 2, h // 2)
                            for tt in range(2):
                                q2 = qsq[h // 2][:, (h % 2) * T + tt * P:(h % 2) * T + (tt + 1) * P]
                                mm = eng.matmul(bank[7][:, 2 * h + tt:2 * h + tt + 1], q2, con_("ones")[:, 0:1],
                                                start=True, stop=True)
                        k.inc("qss", mm)
                    for h in range(4):
                        b = bank[4 + h]
                        k.wait(free[4 + h][0], st, i, *free[4 + h][1:])
                        r, m = slice(HD * (h % 2), HD * (h % 2) + HD), h // 2
                        if kind == "moba":
                            eng.matmul(b[:, 0:P], Q[r, m, 0:P], KB[r, m, 0:P], start=True, stop=True)
                            mm = eng.matmul(b[:, P:384], Q[r, m, P:T], KB[r, m, :], start=True, stop=True)
                        elif kind == "sb":
                            eng.matmul(b[:, 0:T], KB[r, m, 0:P], Q[r, m, :], start=True, stop=True)
                            mm = eng.matmul(b[:, T:384], KB[r, m, P:T], Q[r, m, P:T], start=True, stop=True)
                        else:
                            if h == 3:
                                k.wait("qlr", st, i, 2, 1)
                            if isinstance(i, int):
                                k.wait("kn", st)
                            eng.matmul(b[:, 0:P], Q[:, h, 0:P], kn[:, 0:P], start=True, stop=False,
                                       skip_group_check=True)
                            eng.matmul(b[:, P:384], Q[:, h, P:T], kn, start=False, stop=False, skip_group_check=True)
                            if isinstance(i, int):
                                k.wait("msk", st, b=1)
                            mm = eng.matmul(b[:, 0:384], ident_b, maskb, start=False, stop=True,
                                            skip_group_check=True)
                        k.inc("sc", mm)

                def turn(i, h):
                    k.wait("prb" if kind == "sb" else "prs", st, i, 4, h - 4)
                    name = "arg" if kind == "sb" else "ptc"
                    if h >= 2:
                        k.wait(name, st, i, 4, h - 6)
                    else:
                        k.wait("lg", st, i, 4, 3 - h - 4)
                    b = bank[7 - h % 2]
                    if kind == "sb":
                        keep, triL = LK[:, h, :], con_("triL")
                        eng.matmul(b[:, 0:T], triL, keep[:, 0:T], start=True, stop=False, skip_group_check=True)
                        eng.matmul(b[:, P:T], con_("ones"), keep[:, T:384], start=False, stop=False,
                                   skip_group_check=True)
                        eng.matmul(b[:, T:384], triL, keep[:, T:384], start=False, stop=False, skip_group_check=True)
                        diag = b[:, :].rearrange("p (a b c) -> p a b c", a=2, b=2)[:, :, 0, :]
                        mm = eng.matmul(diag, ident_b, above_b.unsqueeze(1).to_broadcast([P, 2, P]),
                                        start=False, stop=True, skip_group_check=True)
                    else:
                        for c in range(3):
                            mm = eng.transpose(b[:, c * P:(c + 1) * P], S[:, h, c * P:(c + 1) * P], con_("ident"))
                    k.inc("ptp", mm)

                def values(i, p):
                    if kind != "dsa":
                        k.wait("vev", st, i, 1, -1)
                    if p and kind != "dsa":
                        k.wait("alo", st, i, 2, -2)
                    if p and kind == "dsa":
                        k.wait("ol", st, i, 2, -2)
                    for h in (2 * p, 2 * p + 1):
                        k.wait("ptc", st, i, 4, h - 4)
                        pr = PT[:, h % 2, :]
                        if kind == "dsa":
                            d, v = bank[4][:, (h % 2) * T:(h % 2 + 1) * T], [ltok[:, tt, :] for tt in range(2)]
                        else:
                            d = bank[4][HD * (h % 2):HD * (h % 2) + HD, p * T:(p + 1) * T]
                            v = [VB[:, tt, h * HD:(h + 1) * HD] for tt in range(2)]
                        eng.matmul(d, v[0], pr[:, 0:T], start=True, stop=False)
                        mm = eng.matmul(d[:, P:T], v[1], pr[:, T:384], start=False, stop=True)
                    k.inc("pv", mm)

                def lift(i, p):
                    k.wait("ol", st, i, 2, p - 2)
                    k.wait("wu", st, i, 1, -1)
                    if p:
                        k.wait("alo", st, i, 2, -2)
                    for j in range(2):
                        h = 2 * p + j
                        mm = eng.matmul(bank[5][HD * j:HD * j + HD, p * T:(p + 1) * T], wu[:, h * HD:(h + 1) * HD],
                                        OL[:, j, :], start=True, stop=True)
                    k.inc("olc", mm)

                def body(i, loop, a, b, more):
                    k.wait("lg", st, i, 4, -4)
                    gemm(bank[4], st, i, a, b, loop, first=not more and kind != "dsa")
                    if more:
                        turn(i, 0)
                        turn(i, 1)
                    k.wait("lg", st, i, 4, -3)
                    gemm(bank[5], st, i, a, b + 1, loop)
                    if more:
                        k.wait("qev", st, i, 1, 0)
                        values(i, 0)
                        turn(i, 2)
                        turn(i, 3)
                    if kind == "dsa":
                        if more:
                            k.wait("qev2", st, i, 1, 0)
                            lift(i, 0)
                            values(i, 1)
                            lift(i, 1)
                    else:
                        k.wait("kev", st, i, 1, 0)
                        gemm(bank[5], st, i, a, b + 2, loop, tokens=True)
                        if more:
                            values(i, 1)
                    scores(i)
                    if more:
                        gemm_out(st, i, a, b + (2 if kind == "dsa" else 3), loop,
                                 lambda kk: k.wait("alo", st, i, 2, kk - 2))

                if kind == "dsa":
                    sparse_front(st)
                    body(0, None, 0, 3, False)
                    for i in k.loop(1, n):
                        body(i, (1, n), 3, 2, True)
                else:
                    body(0, None, 0, 0, False)
                    for i in k.loop(1, n):
                        body(i, (1, n), 4, -1, True)
                turn(n, 0)
                turn(n, 1)
                values(n, 0)
                turn(n, 2)
                turn(n, 3)
                if kind == "dsa":
                    lift(n, 0)
                    values(n, 1)
                    lift(n, 1)
                else:
                    values(n, 1)
                k.wait("ptc", st, b=4 * n - 1)
                last(st, lambda: k.wait("alo", st, b=2 * n - 1))

            def sparse_front(st):
                gemm(bank[4], st, b=0, first=True)
                k.wait("modv", st)
                for tt in range(2):
                    for kk in range(KT):
                        part, ws = slice(tt * P, (tt + 1) * P), slice(40 * kk + 32, 40 * kk + 40)
                        mm = three(bank[7][:, 8 * tt:8 * tt + 8], h_hi[:, kk, part], h_lo[:, kk, part],
                                   ws_hi[:, ws], ws_lo[:, ws], kk == 0, kk == KT - 1)
                k.inc("wip", mm)
                o, _ = PARAMS["relb"]
                k.inc("relp", eng.matmul(bank[7][0:16, P:512], par[0:32, o:o + 16], con_("onehot", 32),
                                         start=True, stop=True))
                for n in (1, 2):
                    gemm(bank[4 + n], st, b=n)
                    if n == 1:
                        k.wait("relv", st)
                        k.wait("ksq", st)
                        k.inc("kss", eng.matmul(bank[7][:, 0:T], con_("ones"), qsq[0][:, 0:T], start=True, stop=True))
                k.wait("klr", st, b=1)
                for tt in range(2):
                    mm = eng.transpose(bank[7][:, tt * P:(tt + 1) * P], latT[:, tt * P:(tt + 1) * P], con_("ident"))
                k.inc("ltp", mm)
                k.wait("pre", st, b=2)
                for h in range(8):
                    if h >= 2:
                        k.wait("rel", st, b=h - 2)
                    b, r = bank[4 + h % 2], slice(HD * (h % 2), HD * (h % 2) + HD)
                    eng.matmul(b[:, 0:P], Q[r, h // 2, 0:P], ki2[r, 0:P], start=True, stop=True)
                    k.inc("ix", eng.matmul(b[:, P:384], Q[r, h // 2, P:T], ki2[r, :], start=True, stop=True))
                k.wait("rel", st, b=7)

            programs = {"ffn": ffn, "cffn": ffn, "mamba": mamba, "moba": lambda st: heads(st, "moba"),
                        "sb": lambda st: heads(st, "sb"), "dsa": lambda st: heads(st, "dsa")}
            eng.wait_ge(s_con, 16)
            for st, kind in enumerate(stages):
                norm(st)
                programs[kind](st)

        for name, n in plan.total.items():
            assert plan.tally.get(name, 0) == n, (name, plan.tally.get(name, 0), n)


def pack(inp):
    f = {k: np.asarray(v) for k, v in inp.items()}
    blocks = []

    def wide(w):
        n = w.shape[1] // 256
        return w.reshape(KT, P, n, 256).transpose(2, 1, 0, 3).reshape(n, P, 2048)

    def deep(w):
        n = w.shape[0] // 256
        return w.reshape(n, 2, P, D).transpose(0, 2, 1, 3).reshape(n, P, 2048)

    def pipelined(front, outs):
        n = len(outs)
        for i in range(n):
            blocks.extend(fr[i] for fr in front)
            if i:
                blocks.append(outs[i - 1])
        blocks.append(outs[n - 1])

    def ffn(i, j):
        pipelined([wide(f["ffn_w_gate"][i, j]), wide(f["ffn_w_up"][i, j])], deep(f["ffn_w_down"][i, j]))

    def cffn(i):
        w = f["ffn_w_up_2"][i]
        pipelined([wide(w[:, :DFF]), wide(w[:, DFF:])], deep(f["ffn_w_down_2"][i]))

    def attn(w, wo):
        pipelined([wide(w[:, :D]), wide(w[:, D:2 * D]), wide(w[:, 2 * D:])], deep(wo))

    def mamba():
        w = f["ssm_w_in"][0]
        z, xs, bm, cm = w[:, :2048], w[:, 2048:4096], w[:, 4096:5120], w[:, 5120:6144]
        bc = np.concatenate([bm.reshape(D, 8, P), cm.reshape(D, 8, P)], 2).reshape(D, 2048)
        pipelined([wide(xs), wide(bc), wide(z)], deep(f["ssm_w_out"][0]))

    def dsa():
        w = f["dsa_w_in_2"][0]
        q, lat, qi, ki = w[:, :2048], w[:, 2048:2176], w[:, 2176:2688], w[:, 2688:2752]
        blocks.extend(wide(np.concatenate([lat, ki, ki, qi], 1)))
        qb = wide(q)
        pipelined([qb[0::2], qb[1::2]], deep(f["dsa_w_out_2"][0]))

    ffn(0, 0)
    mamba()
    ffn(0, 1)
    ffn(1, 0)
    attn(f["attn_w_qkv"][0], f["attn_w_out"][0])
    ffn(1, 1)
    attn(f["sb_w_in_2"][0], f["sb_w_out_2"][0])
    cffn(0)
    dsa()
    cffn(1)
    weights = np.ascontiguousarray(np.stack(blocks))

    mods = np.concatenate([f["mod_w"].reshape(6, D, 3 * D),
                           f["ada_w_2"].reshape(2, D, 2, 3 * D).transpose(0, 2, 1, 3).reshape(4, D, 3 * D)])
    mods = mods.reshape(NJOB * KT, P, 3 * D)

    def col(v):
        return v.reshape(-1, P).T

    params = np.zeros((P, NPARAM), np.float32)

    def put(name, v):
        at, n = PARAMS[name]
        params[:v.shape[0], at:at + n] = v

    put("c", np.concatenate([col(f["c"][0])] * 6 + [col(f["c_2"][0])] * 4, 1))
    g2 = np.stack([f["norm_mix_2"], f["norm_ffn_2"]], 1).reshape(4, D)
    put("g", col(np.concatenate([f["norm_g"].reshape(6, D), g2])))
    put("gfin", col(f["final_norm_g"]))
    put("modb", col(np.concatenate([f["mod_b"].reshape(6, 3 * D), f["ada_b_2"].reshape(4, 3 * D)])))
    small = np.concatenate([f["ssm_w_in"][0][:, 6144:], f["dsa_w_in_2"][0][:, 2752:]], 1)
    put("wsmall", small.reshape(KT, P, 40).transpose(1, 0, 2).reshape(P, 320))
    put("dtb", np.broadcast_to(f["ssm_dt_bias"][0], (P, 32)))
    put("alog", np.broadcast_to(f["ssm_a_log"][0], (P, 32)))
    cw = np.concatenate([f["ssm_conv_w"][0][:, 0, :], f["ssm_conv_b"]]).reshape(5, 32, P)
    order = [t for g in range(8) for t in (2 * g, 2 * g + 1, 16 + g, 24 + g)]
    put("cw", cw[:, order, :].transpose(2, 1, 0).reshape(P, 160))
    put("dskip", col(np.repeat(f["ssm_d"][0], HD)))
    put("ngw", col(f["ssm_norm_w"][0]))
    fc = np.concatenate([f["ffn_conv_w_2"], f["ffn_conv_b_2"][:, None, :]], 1).reshape(2, 4, 44, P)
    put("fcw", fc.transpose(3, 0, 2, 1).reshape(P, 352))
    put("qn", f["dsa_q_norm_2"].T)
    put("kn", f["dsa_k_norm_2"].T)
    put("wuv", f["dsa_w_uv_2"][0].transpose(1, 0, 2).reshape(P, 1024))
    put("relb", f["rel_bias_2"])
    xin = f["x"][0].T.reshape(KT, P, T).transpose(1, 0, 2)
    return {"weights": weights, "mods": np.ascontiguousarray(mods), "params": params, "consts": constants(),
            "xin": np.ascontiguousarray(xin)}


def kernel(**inputs):
    import concourse.bacc as _bacc
    from concourse.bass_utils import run_bass_kernel_spmd as _run

    arrays = pack(inputs)
    nc = _bacc.Bacc("TRN2", target_bir_lowering=False, num_devices=1)
    args = [nc.dram_tensor(n, a.shape, F32, kind="ExternalInput").ap() for n, a in arrays.items()]
    out = nc.dram_tensor("out", (P, KT, T), F32, kind="ExternalOutput").ap()
    build(nc, *args, out)
    r = _run(nc, [arrays], core_ids=[0])
    got = r.results[0]["out"]
    return np.ascontiguousarray(got.transpose(2, 1, 0).reshape(1, T, D))
```
